# Optimizing a Trainium2 kernel written in Bass

```python
import math
import jax, jax.numpy as jnp
from jax import lax
import numpy as np

D_MODEL = 1024
BATCH = 1
SEQ = 1024
DEPTH = 2

N_META = 16
N_A_LAYERS = DEPTH // 2
N_B_LAYERS = DEPTH - N_A_LAYERS
SSM_GROUP = 16
SSM_GROUPS = D_MODEL // SSM_GROUP
SSM_STATE = 64
DT_MIN = 1e-3
DT_MAX = 1e-1
HEAD_DIM = 64
N_Q_HEADS = D_MODEL // HEAD_DIM
N_KV_HEADS = 4
GQA_GROUP = N_Q_HEADS // N_KV_HEADS
KV_DIM = N_KV_HEADS * HEAD_DIM
WINDOW = 128
BLOCK = 128
PAD_FRONT = BLOCK - N_META
NEG = -1e30
N_EXPERT_GROUPS = 4
EXPERTS_PER_GROUP = 8
N_EXPERTS = N_EXPERT_GROUPS * EXPERTS_PER_GROUP
TOP_K = 2
D_EXPERT = D_MODEL // 2
MOE_BLOCK = 128
RMS_EPS = 1e-6

kernel_name = 'yoco_s5_swa_sink_hier_moe'

F32 = jnp.float32

def rmsnorm(x, g):
    xf = x.astype(F32)
    y = xf * lax.rsqrt(jnp.mean(xf * xf, axis=-1, keepdims=True) + RMS_EPS)
    return (y * g.astype(F32)).astype(x.dtype)

def s5_mixer(u, a_re, a_im, log_dt, b_re, b_im, c_re, c_im, d_skip, w_glu):
    bsz, L, _ = u.shape
    uf = u.astype(F32)
    ug = uf.reshape(bsz, L, SSM_GROUPS, SSM_GROUP).astype(jnp.complex64)
    lam = lax.complex(a_re.astype(F32), a_im.astype(F32))
    dt = jnp.exp(log_dt.astype(F32))[:, None]
    a_bar = jnp.exp(lam * dt)
    b = lax.complex(b_re.astype(F32), b_im.astype(F32))
    b_bar = ((a_bar - 1.0) / lam)[:, :, None] * b
    bu = jnp.einsum('blgc,gpc->blgp', ug, b_bar)
    a_seq = jnp.broadcast_to(a_bar, bu.shape)

    def combine(e1, e2):
        a1, s1 = e1
        a2, s2 = e2
        return a2 * a1, a2 * s1 + s2

    _, states = lax.associative_scan(combine, (a_seq, bu), axis=1)
    c = lax.complex(c_re.astype(F32), c_im.astype(F32))
    y = jnp.einsum('blgp,gcp->blgc', states, c).real.reshape(bsz, L, D_MODEL)
    z = jax.nn.gelu(y + d_skip.astype(F32) * uf).astype(u.dtype)
    val, gate = jnp.split(z @ w_glu, 2, axis=-1)
    return val * jax.nn.sigmoid(gate)

def to_blocks(t):
    t = jnp.pad(t, ((0, 0), (PAD_FRONT, 0)) + ((0, 0),) * (t.ndim - 2))
    return t.reshape((t.shape[0], t.shape[1] // BLOCK, BLOCK) + t.shape[2:])

def band_keys(tb):
    prev = jnp.pad(tb, ((0, 0), (1, 0), (0, 0), (0, 0), (0, 0)))[:, :-1]
    return jnp.concatenate([prev, tb], axis=2)

def shared_kv(h, w_kv, b_kv):
    bsz, L, _ = h.shape
    k, v = jnp.split(h @ w_kv + b_kv, 2, axis=-1)
    k = k.reshape(bsz, L, N_KV_HEADS, HEAD_DIM)
    v = v.reshape(bsz, L, N_KV_HEADS, HEAD_DIM)
    k_band = band_keys(to_blocks(k))
    v_band = band_keys(to_blocks(v))
    return k_band, v_band, k[:, :N_META], v[:, :N_META]

def swa_sink_attention(h, w_q, b_q, sinks, w_o, b_o, k_band, v_band, k_meta, v_meta):
    bsz, L, _ = h.shape
    q = (h @ w_q + b_q).reshape(bsz, L, N_KV_HEADS, GQA_GROUP, HEAD_DIM)
    qb = to_blocks(q)
    nb = qb.shape[1]
    scale = HEAD_DIM ** -0.5
    s_band = jnp.einsum('bnqkgd,bnskd->bnkgqs', qb, k_band).astype(F32) * scale
    s_meta = jnp.einsum('bnqkgd,bmkd->bnkgqm', qb, k_meta).astype(F32) * scale
    qpos = jnp.arange(nb)[:, None] * BLOCK + jnp.arange(BLOCK)[None, :]
    kpos = jnp.arange(nb)[:, None] * BLOCK - BLOCK + jnp.arange(2 * BLOCK)[None, :]
    diff = qpos[:, :, None] - kpos[:, None, :]
    band_ok = (kpos[:, None, :] >= BLOCK) & (diff >= 0) & (diff < WINDOW)
    mpos = PAD_FRONT + jnp.arange(N_META)
    meta_ok = mpos[None, None, :] <= qpos[:, :, None]
    s_band = jnp.where(band_ok[None, :, None, None], s_band, NEG)
    s_meta = jnp.where(meta_ok[None, :, None, None], s_meta, NEG)
    sink = sinks.astype(F32).reshape(1, 1, N_KV_HEADS, GQA_GROUP, 1, 1)
    sink = jnp.broadcast_to(sink, s_meta.shape[:-1] + (1,))
    probs = jax.nn.softmax(jnp.concatenate([sink, s_meta, s_band], axis=-1), axis=-1)
    p_meta = probs[..., 1:1 + N_META].astype(v_band.dtype)
    p_band = probs[..., 1 + N_META:].astype(v_band.dtype)
    o = (jnp.einsum('bnkgqm,bmkd->bnqkgd', p_meta, v_meta)
         + jnp.einsum('bnkgqs,bnskd->bnqkgd', p_band, v_band))
    o = o.reshape(bsz, nb * BLOCK, D_MODEL)[:, PAD_FRONT:]
    return o @ w_o + b_o

def hier_moe(h, w_grp, b_grp, w_exp, b_exp, w_gate, w_up, w_down):
    bsz, L, D = h.shape
    t = h.reshape(-1, D)
    T = t.shape[0]
    grp_prob = jax.nn.softmax((t @ w_grp + b_grp).astype(F32), axis=-1)
    p_g, g_idx = lax.top_k(grp_prob, 1)
    exp_logits = (t @ w_exp + b_exp).astype(F32).reshape(T, N_EXPERT_GROUPS, EXPERTS_PER_GROUP)
    sel_idx = jnp.broadcast_to(g_idx[:, :, None], (T, 1, EXPERTS_PER_GROUP))
    sel_logits = jnp.take_along_axis(exp_logits, sel_idx, axis=1)[:, 0]
    q_top, e_local = lax.top_k(jax.nn.softmax(sel_logits, axis=-1), TOP_K)
    q_top = q_top / jnp.sum(q_top, axis=-1, keepdims=True)
    gates = p_g * q_top
    experts = g_idx * EXPERTS_PER_GROUP + e_local
    n_assign = T * TOP_K
    flat_e = experts.reshape(-1)
    flat_tok = jnp.repeat(jnp.arange(T), TOP_K)
    flat_gate = gates.reshape(-1)
    order = jnp.argsort(flat_e)
    se = flat_e[order]
    stok = flat_tok[order]
    sgate = flat_gate[order]
    counts = jnp.bincount(flat_e, length=N_EXPERTS)
    padded = (counts + MOE_BLOCK - 1) // MOE_BLOCK * MOE_BLOCK
    pad_end = jnp.cumsum(padded)
    pad_start = pad_end - padded
    start = jnp.cumsum(counts) - counts
    dest = pad_start[se] + jnp.arange(n_assign) - start[se]
    n_rows = (n_assign // MOE_BLOCK + 1 + N_EXPERTS) * MOE_BLOCK
    n_blk = n_rows // MOE_BLOCK
    row_tok = jnp.full((n_rows,), T, dtype=jnp.int32).at[dest].set(stok)
    t_pad = jnp.concatenate([t, jnp.zeros((1, D), t.dtype)], axis=0)
    xb = t_pad[row_tok].reshape(n_blk, MOE_BLOCK, D)
    blk_e = jnp.minimum(jnp.searchsorted(pad_end, jnp.arange(n_blk) * MOE_BLOCK, side='right'),
                        N_EXPERTS - 1)

    def run_block(args):
        xblk, e = args
        hid = jax.nn.silu(xblk @ w_gate[e]) * (xblk @ w_up[e])
        return hid @ w_down[e]

    yb = lax.map(run_block, (xb, blk_e)).reshape(n_rows, D)
    contrib = yb[dest] * sgate[:, None].astype(yb.dtype)
    out = jnp.zeros_like(t).at[stok].add(contrib)
    return out.reshape(bsz, L, D)

def setup_inputs(seed: int = 0) -> dict:
    key = jax.random.key(seed)
    ks = iter(jax.random.split(key, 40))
    nrm = lambda shape, s: jax.random.normal(next(ks), shape, F32) * s
    G, P, C = SSM_GROUPS, SSM_STATE, SSM_GROUP
    a_im0 = jnp.pi * jnp.arange(P, dtype=F32)
    return {
        'x': nrm((BATCH, SEQ, D_MODEL), 1.0),
        'meta_tokens': nrm((N_META, D_MODEL), 1.0),
        'norm_mix': 1.0 + nrm((DEPTH, D_MODEL), 0.02),
        'norm_ffn': 1.0 + nrm((DEPTH, D_MODEL), 0.02),
        'norm_kv': 1.0 + nrm((D_MODEL,), 0.02),
        'norm_final': 1.0 + nrm((D_MODEL,), 0.02),
        'ssm_a_re': -0.5 * jnp.exp(nrm((N_A_LAYERS, G, P), 0.05)),
        'ssm_a_im': a_im0 + nrm((N_A_LAYERS, G, P), 0.01),
        'ssm_log_dt': jax.random.uniform(next(ks), (N_A_LAYERS, G), F32,
                                         minval=math.log(DT_MIN), maxval=math.log(DT_MAX)),
        'ssm_b_re': nrm((N_A_LAYERS, G, P, C), (2 * C) ** -0.5),
        'ssm_b_im': nrm((N_A_LAYERS, G, P, C), (2 * C) ** -0.5),
        'ssm_c_re': nrm((N_A_LAYERS, G, C, P), P ** -0.5),
        'ssm_c_im': nrm((N_A_LAYERS, G, C, P), P ** -0.5),
        'ssm_d': nrm((N_A_LAYERS, D_MODEL), 1.0),
        'ssm_w_glu': nrm((N_A_LAYERS, D_MODEL, 2 * D_MODEL), D_MODEL ** -0.5),
        'w_kv': nrm((D_MODEL, 2 * KV_DIM), D_MODEL ** -0.5),
        'b_kv': nrm((2 * KV_DIM,), 0.01),
        'w_q': nrm((N_B_LAYERS, D_MODEL, D_MODEL), D_MODEL ** -0.5),
        'b_q': nrm((N_B_LAYERS, D_MODEL), 0.01),
        'attn_sinks': nrm((N_B_LAYERS, N_Q_HEADS), 1.0),
        'w_o': nrm((N_B_LAYERS, D_MODEL, D_MODEL), D_MODEL ** -0.5),
        'b_o': nrm((N_B_LAYERS, D_MODEL), 0.01),
        'moe_w_grp': nrm((DEPTH, D_MODEL, N_EXPERT_GROUPS), D_MODEL ** -0.5),
        'moe_b_grp': nrm((DEPTH, N_EXPERT_GROUPS), 0.01),
        'moe_w_exp': nrm((DEPTH, D_MODEL, N_EXPERTS), D_MODEL ** -0.5),
        'moe_b_exp': nrm((DEPTH, N_EXPERTS), 0.01),
        'moe_w_gate': nrm((DEPTH, N_EXPERTS, D_MODEL, D_EXPERT), D_MODEL ** -0.5),
        'moe_w_up': nrm((DEPTH, N_EXPERTS, D_MODEL, D_EXPERT), D_MODEL ** -0.5),
        'moe_w_down': nrm((DEPTH, N_EXPERTS, D_EXPERT, D_MODEL), D_EXPERT ** -0.5),
    }

def reference(x, meta_tokens, norm_mix, norm_ffn, norm_kv, norm_final,
              ssm_a_re, ssm_a_im, ssm_log_dt, ssm_b_re, ssm_b_im, ssm_c_re, ssm_c_im,
              ssm_d, ssm_w_glu, w_kv, b_kv, w_q, b_q, attn_sinks, w_o, b_o,
              moe_w_grp, moe_b_grp, moe_w_exp, moe_b_exp, moe_w_gate, moe_w_up, moe_w_down):
    bsz = x.shape[0]
    meta = jnp.broadcast_to(meta_tokens[None].astype(x.dtype), (bsz, N_META, D_MODEL))
    h = jnp.concatenate([meta, x], axis=1)
    shared = None
    for layer in range(DEPTH):
        if layer < N_A_LAYERS:
            i = layer
            h = h + s5_mixer(rmsnorm(h, norm_mix[layer]), ssm_a_re[i], ssm_a_im[i], ssm_log_dt[i],
                             ssm_b_re[i], ssm_b_im[i], ssm_c_re[i], ssm_c_im[i],
                             ssm_d[i], ssm_w_glu[i])
        else:
            if shared is None:
                shared = shared_kv(rmsnorm(h, norm_kv), w_kv, b_kv)
            j = layer - N_A_LAYERS
            k_band, v_band, k_meta, v_meta = shared
            h = h + swa_sink_attention(rmsnorm(h, norm_mix[layer]), w_q[j], b_q[j], attn_sinks[j],
                                       w_o[j], b_o[j], k_band, v_band, k_meta, v_meta)
        h = h + hier_moe(rmsnorm(h, norm_ffn[layer]), moe_w_grp[layer], moe_b_grp[layer],
                         moe_w_exp[layer], moe_b_exp[layer], moe_w_gate[layer],
                         moe_w_up[layer], moe_w_down[layer])
    h = rmsnorm(h, norm_final)
    return h[:, N_META:]


_drawn_inputs = setup_inputs


def setup_inputs(seed=0):
    import zlib

    import numpy as np

    out = dict(_drawn_inputs(seed))
    spreads = {}
    factors = {'norm_kv': 3.253,
     'norm_final': 7.325,
     'ssm_a_re': 39.04,
     'b_q': 6.917,
     'attn_sinks': 5.462,
     'b_kv': 6.367,
     'b_o': 5.643}
    for name, (base, spread) in spreads.items():
        noise = np.random.default_rng([zlib.crc32(name.encode()), seed]).standard_normal(out[name].shape)
        drawn = base * np.exp(spread * noise) if base else spread * noise
        out[name] = __import__('jax').numpy.asarray(drawn.astype(out[name].dtype))
    for name, factor in factors.items():
        out[name] = (out[name] * factor).astype(out[name].dtype)
    return out
```

```python
import math
from contextlib import ExitStack

import numpy as np

import concourse.bass as bass
from concourse import mybir

F32 = mybir.dt.float32
F32R = mybir.dt.float32r
I32 = mybir.dt.int32
U32 = mybir.dt.uint32
ALU = mybir.AluOpType
ACT = mybir.ActivationFunctionType
AX = mybir.AxisListType

D = 1024
SEQ = 1024
N_META = 16
T_ALL = SEQ + N_META
P = 128
DC = D // P
XT = SEQ // P
EPS = 1e-6

G = 64
C = 16
S = 64
J = G // 2
L = 8
NCH = T_ALL // L
BLK = 13
NBLK = NCH // BLK
HW = (2 * L - 1) * C

LOG2E = 1.4426950408889634
LN2_A, LN2_B = 0.693359375, -2.12194440e-4
TWO_PI_A = 6.28125
TWO_PI_B = 2 * math.pi - TWO_PI_A
ROUND = 12582912.0
FACT = [1.0 / math.factorial(n) for n in range(8)]


def tile_rows(i):
    return P if i < XT else N_META


def tile_chunk0(i):
    return N_META // L + i * (P // L) if i < XT else 0


def semaphore_source(nc, ctx, prefix):
    sems = []

    def clear():
        nc.clear_and_free_semaphores(sems)
        nc.all_engine_barrier()

    def sem(name):
        sems.append(nc.alloc_semaphore(name=prefix + name))
        return sems[-1]

    ctx.callback(clear)
    return sem


def make_identity(nc, pool, ident, sem):
    nc.gpsimd.memset(ident[:], 0.0).then_inc(sem, 1)
    pool.wait_ge(sem, 1)
    nc.gpsimd.affine_select(out=ident[:], in_=ident[:], compare_op=ALU.not_equal, fill=1.0, base=0,
                            pattern=[[-1, P]], channel_multiplier=1).then_inc(sem, 1)


def phase_ssm(nc, t):
    NT = XT + 1
    W = BLK - 1
    NH = G // 4
    NY = 2 * -(-J // 3)
    POOL_BLOCKS = (3, 6, 9)
    JC = J * C
    with ExitStack() as ctx:
        def sb(name, shape, dt=F32):
            return ctx.enter_context(nc.sbuf_tensor("ssm_" + name, shape, dt))

        sem = semaphore_source(nc, ctx, "ssm_")

        ident = sb("ident", [P, P])
        reg1 = sb("reg1", [P, G * NCH])
        v_re = reg1[:, 0:L * JC].rearrange("p (j k c) -> p j k c", k=L, c=C)
        v_im = reg1[:, L * JC:2 * L * JC].rearrange("p (j k c) -> p j k c", k=L, c=C)
        z = reg1[:, :].rearrange("p (g n) -> p g n", g=G)
        reg2 = sb("reg2", [P, 2 * J * (NCH + 1)])
        lam = reg2[0:J, 0:20 * P].rearrange("p (q m) -> p q m", q=20)
        pb_r, pb_i = (reg2[:, 2560 + q * BLK * J:2560 + (q + 1) * BLK * J].rearrange("p (k j) -> p k j", j=J)
                      for q in range(2))
        ptmp = reg2[:, 4096:4096 + L * J].rearrange("p (k j) -> p k j", j=J)
        tmp = reg2[:, 0:(L + 1) * JC].rearrange("p (j k c) -> p j k c", k=L + 1, c=C)
        st = reg2[:, :].rearrange("p (a n) -> p a n", n=NCH + 1)
        st4 = reg2[:, :].rearrange("p (q j n) -> p q j n", q=2, j=J)
        reg3 = sb("reg3", [P, G * NCH])
        ut = reg3[:, :].rearrange("p (c s n) -> p c s n", c=DC, s=L)
        tm = reg3[:, 0:G * P].rearrange("p (g m) -> p g m", g=G)
        ca_x = reg3[:, 0:(L + 1) * JC]
        bb_st = reg3[:, (L + 1) * JC:(L + 3) * JC].rearrange("p (r j c) -> p r j c", r=2, c=C)
        ca_t = reg3[:, (L + 3) * JC:(L + 3) * JC + (L + 1) * JC // 8].rearrange(
            "p (j k c) -> p j k c", k=L + 1, c=C)
        reg4 = sb("reg4", [P, G * NCH])
        uc = reg4[:, :].rearrange("p (g n) -> p g n", g=G)
        xin = reg4[:, 0:2 * D].rearrange("p (b d) -> p b d", b=2)
        xn = reg4[:, 2 * D:4 * D].rearrange("p (b d) -> p b d", b=2)
        gmix = reg4[:, 4 * D:5 * D]
        sq = reg4[:, 5 * D:6 * D]
        CW = 6 * J * W
        reg5 = sb("reg5", [P, 2 * CW])
        b_re, b_im, bb_re, bb_im, c_re, c_im = (
            reg5[:, q * JC:(q + 1) * JC].rearrange("p (j c) -> p j c", c=C) for q in range(6))
        c_raw = reg5[:, 6 * JC:8 * JC].rearrange("p (a q m) -> p a q m", a=2, q=4)
        dd = reg5[0:C, 6 * JC:8 * JC].rearrange("p (g c) -> p g c", c=C)
        st_x = reg5[:, 0:J * NCH].rearrange("p (j n) -> p j n", n=NCH)
        pw_r, pw_i, pw_n = (sb(f"pw_{x}", [P, L + 1, J]) for x in "rin")
        ca_re, ca_ni = (sb(f"ca_{x}", [P, J, L + 1, C]) for x in ("re", "ni"))
        rot = sb("rot", [P, 2, 2, J, BLK])
        hbuf = sb("hbuf", [C, 2, 4, HW])
        dcol = sb("dcol", [C, G])
        vt = sb("vt", [P, 2, 2 * P])
        kint = sb("kint", [J, P], I32)
        ldt = sb("ldt", [J, 2])
        halfpi = sb("halfpi", [P, 1])
        mhalf = sb("mhalf", [P, 1])
        ptiny = sb("ptiny", [1, 1])
        ss = sb("ss", [P, NT])
        rstd = sb("rstd", [P, NT])
        pst = ctx.enter_context(nc.psum_tensor("ssm_pst", [P, 2, D], F32))
        psr = ctx.enter_context(nc.psum_tensor("ssm_psr", [P, 4, 512], F32))

        x_in = [sem(f"x_in{b}") for b in range(2)]
        gmix_in, lam_in, b_in, c_in, ut_out, uc_in, tm_in, z_out = (
            sem(x) for x in ("gmix_in", "lam_in", "b_in", "c_in", "ut_out", "uc_in", "tm_in", "z_out"))
        h_out = [sem(f"h_out{b}") for b in range(2)]
        ident_step, consts_set, pads_set, pool_step, dve_step = (
            sem(x) for x in ("ident_step", "consts_set", "pads_set", "pool_step", "dve_step"))
        squares_done, rstd_done, xn_done, xt_done, ut_done = (
            sem(x) for x in ("squares_done", "rstd_done", "xn_done", "xt_done", "ut_done"))
        angle_ready, trig_done, aq_ready, aq_t, ct_done, c_copied = (
            sem(x) for x in ("angle_ready", "trig_done", "aq_ready", "aq_t", "ct_done", "c_copied"))
        powers_done, bbar_done, ca_done, v_prod, v_done = (
            sem(x) for x in ("powers_done", "bbar_done", "ca_done", "v_prod", "v_done"))
        h_mm, h_copied, vt_mm, vt_done, x_mm, st_in, st_done = (
            sem(x) for x in ("h_mm", "h_copied", "vt_mm", "vt_done", "x_mm", "st_in", "st_done"))
        slot0_set, carries_done, corr_pool, y_mm, z_done = (
            sem(x) for x in ("slot0_set", "carries_done", "corr_pool", "y_mm", "z_done"))
        ca_crossed, ca_stacked, st_crossed, st_stacked = (
            sem(x) for x in ("ca_crossed", "ca_stacked", "st_crossed", "st_stacked"))

        def h_groups(q):
            g0 = 8 * (q // 2) + q % 2
            return slice(g0, g0 + 7, 2)

        def y_groups(y):
            g0 = 6 * (y // 2) + y % 2
            return list(range(g0, min(g0 + 5, G), 2))

        u_dram, h_dram, z_dram = t["u_dram"], t["h_dram"], t["z_dram"]
        block = ctx.enter_context(nc.Block())

        @block.sync
        def _(sp):
            for q, src in enumerate((t["ssm_a_re"][0], t["ssm_a_im"][0])):
                sp.dma_start(lam[:, q, :], src.rearrange("(j r) p -> j (r p)", r=2)).then_inc(lam_in, 16)
            sp.dma_start(ldt[:, :], t["ssm_log_dt"][0].rearrange("(j r) -> j r", r=2)).then_inc(lam_in, 16)
            sp.dma_start(gmix, t["norm_mix"][0].partition_broadcast(P)).then_inc(gmix_in, 16)
            for i in range(2):
                sp.dma_start(xin[:, i, :], t["x"][0, i * P:(i + 1) * P, :]).then_inc(x_in[i], 16)
            for part, src in enumerate((t["ssm_c_re"][0], t["ssm_c_im"][0])):
                for q in range(4):
                    for r in range(2):
                        sp.dma_start(c_raw[:, part, q, r * S:(r + 1) * S],
                                     src.rearrange("(q j r) c p -> q r j c p", q=4, r=2)[q, r]).then_inc(c_in, 16)
            for dst, src in ((b_re, t["ssm_b_re"][0]), (b_im, t["ssm_b_im"][0])):
                for r in range(2):
                    sp.dma_start(dst[r * S:(r + 1) * S],
                                 src.rearrange("(j r) p c -> r p j c", r=2)[r]).then_inc(b_in, 16)
            sp.dma_start(dcol[:, :], t["ssm_d"][0].rearrange("(g c) -> c g", c=C),
                         allow_slow_non_contiguous=True).then_inc(b_in, 16)
            for i in range(2, NT):
                sp.wait_ge(xn_done, i - 1)
                src = t["x"][0, i * P:(i + 1) * P, :] if i < XT else t["meta_tokens"]
                sp.dma_start(xin[0:tile_rows(i), i % 2, :], src).then_inc(x_in[i % 2], 16)
            sp.wait_ge(ut_done, 2 * NT)
            for c in range(DC):
                sp.dma_start(u_dram[c * P:(c + 1) * P], ut[:, c]).then_inc(ut_out, 16)
            sp.wait_ge(ut_out, 16 * DC)
            for q in range(L):
                sp.dma_start(uc[q * C:(q + 1) * C],
                             u_dram.rearrange("(g c) s n -> s c g n", c=C)[L - 1 - q]).then_inc(uc_in, 16)
            lo_half, hi_half = slice(0, S), slice(S, P)
            sp.wait_ge(ca_done, 1)
            sp.dma_start(ca_x[lo_half], ca_re[hi_half].rearrange("p j k c -> p (j k c)")).then_inc(ca_crossed, 16)
            sp.wait_ge(bbar_done, 2)
            for r, half in enumerate((lo_half, hi_half)):
                sp.dma_start(bb_st[lo_half, r], bb_re[half]).then_inc(ca_crossed, 16)
                sp.dma_start(bb_st[hi_half, r], bb_im[half]).then_inc(ca_crossed, 16)
            sp.wait_ge(ca_done, 2)
            sp.dma_start(ca_x[hi_half], ca_ni[lo_half].rearrange("p j k c -> p (j k c)")).then_inc(ca_crossed, 16)
            for q in range(NH):
                sp.wait_ge(h_copied, q + 1)
                sp.dma_start(h_dram[:, h_groups(q), :], hbuf[:, q % 2]).then_inc(h_out[q % 2], 16)
            for b in range(2):
                sp.wait_ge(h_out[b], 16 * NH // 2)
            for q in range(L):
                sp.dma_start(tm[q * C:(q + 1) * C], h_dram[:, :, q * C:q * C + P]).then_inc(tm_in, 16)
            sp.wait_ge(st_done, 1)
            sp.wait_ge(corr_pool, len(POOL_BLOCKS))
            sp.wait_ge(slot0_set, 1)
            sp.dma_start(st_x[lo_half], st4[hi_half, 0, :, 0:NCH]).then_inc(st_crossed, 16)
            sp.dma_start(st_x[hi_half], st4[lo_half, 1, :, 0:NCH]).then_inc(st_crossed, 16)
            for half in range(2):
                g0, g1 = half * (G // 2), (half + 1) * (G // 2)
                sp.wait_ge(z_done, min(NY, 2 * -(-g1 // 6)))
                for s in range(L):
                    sp.dma_start(z_dram.rearrange("(g c) s n -> s c g n", c=C)[s][:, g0:g1],
                                 z[s * C:(s + 1) * C, g0:g1]).then_inc(z_out, 16)
            sp.wait_ge(z_out, 16 * 2 * L)

        @block.gpsimd
        def _(pool):
            nc.gpsimd.memset(mhalf[:], -0.5).then_inc(consts_set, 1)
            nc.gpsimd.memset(halfpi[:], math.pi / 2).then_inc(consts_set, 1)
            make_identity(nc, pool, ident, ident_step)
            nc.gpsimd.memset(hbuf[:], 0.0).then_inc(pads_set, 1)
            pool.wait_ge(consts_set, 2)
            for i in range(NT):
                n = tile_rows(i)
                pool.wait_ge(squares_done, i + 1)
                nc.gpsimd.tensor_scalar(ss[0:n, i:i + 1], ss[0:n, i:i + 1], 1.0 / D, EPS,
                                        ALU.mult, ALU.add).then_inc(pool_step, 1)
                pool.wait_ge(pool_step, i + 1)
                nc.gpsimd.tensor_tensor(rstd[0:n, i:i + 1], ss[0:n, i:i + 1], mhalf[0:n, :],
                                        ALU.pow).then_inc(rstd_done, 1)
            pool.wait_ge(powers_done, 1)
            pool.wait_ge(bbar_done, 2)
            for k in range(L):
                for dst, b in ((v_re, bb_re), (v_im, bb_im)):
                    last = nc.gpsimd.tensor_tensor(dst[:, :, k, :], b,
                                                   pw_r[:, k, :].unsqueeze(2).to_broadcast([P, J, C]), ALU.mult)
                last.then_inc(v_prod, 1)
            pool.wait_ge(ca_crossed, 16 * 6)
            nc.gpsimd.tensor_copy(ca_ni[0:S].rearrange("p j k c -> p (j k c)"), ca_x[0:S]).then_inc(ca_stacked, 1)
            pool.wait_ge(h_mm, NH)
            pool.wait_ge(carries_done, 1)
            step = NT
            pr = reg5[:, CW:CW + 4 * J * W].rearrange("p (q a j i) -> p q a j i", q=2, a=2, i=W)
            sm = reg5[:, CW + 4 * J * W:2 * CW].rearrange("p (q j i) -> p q j i", q=2, i=W)
            for b in POOL_BLOCKS:
                for q in range(2):
                    for a in range(2):
                        last = nc.gpsimd.tensor_tensor(
                            pr[:, q, a], rot[:, q, a, :, 0:W],
                            st4[:, a, :, b * BLK:b * BLK + 1].to_broadcast([P, J, W]), ALU.mult)
                last.then_inc(pool_step, 1)
                pool.wait_ge(pool_step, step + 1)
                for q in range(2):
                    last = nc.gpsimd.tensor_tensor(sm[:, q], pr[:, q, 0], pr[:, q, 1], ALU.add)
                last.then_inc(pool_step, 1)
                pool.wait_ge(pool_step, step + 2)
                for q in range(2):
                    dst = st4[:, q, :, 1 + b * BLK:1 + b * BLK + W]
                    last = nc.gpsimd.tensor_tensor(dst, dst, sm[:, q], ALU.add)
                last.then_inc(corr_pool, 1)
                step += 2

        @block.scalar
        def _(act):
            act.wait_ge(consts_set, 2)
            act.wait_ge(angle_ready, 1)
            nc.scalar.activation(lam[:, 10, :], lam[:, 5, :], ACT.Sin, scale=0.5).then_inc(trig_done, 1)
            nc.scalar.activation(lam[:, 11, :], lam[:, 5, :], ACT.Sin, scale=0.5,
                                 bias=halfpi[0:J, :]).then_inc(trig_done, 1)
            act.wait_ge(ct_done, 1)
            for part, dst in enumerate((c_re, c_im)):
                nc.scalar.copy(dst.rearrange("p j c -> p (j c)"), psr[:, part, :]).then_inc(c_copied, 1)

            def squares(i):
                n = tile_rows(i)
                act.wait_ge(x_in[i % 2], 16 * (i // 2 + 1))
                if i:
                    act.wait_ge(squares_done, i)
                nc.scalar.activation(sq[0:n], xin[0:n, i % 2, :], ACT.Square,
                                     accum_out=ss[0:n, i:i + 1]).then_inc(squares_done, 1)

            def store_transposed(i):
                n, n0 = tile_rows(i), tile_chunk0(i)
                act.wait_ge(xt_done, i + 1)
                for h in range(2):
                    src = pst[:, i % 2, 512 * h:512 * h + 4 * P].rearrange("p (c m) -> p c m", c=4)[:, :, 0:n]
                    src = src.rearrange("p c (n s) -> p c s n", s=L)
                    for c in range(4):
                        last = nc.scalar.copy(ut[:, 4 * h + c, :, n0:n0 + n // L], src[:, c])
                    last.then_inc(ut_done, 1)

            squares(0)
            for i in range(NT):
                if i + 1 < NT:
                    squares(i + 1)
                store_transposed(i)
            act.wait_ge(v_done, 2)
            for j in range(J):
                act.wait_ge(x_mm, j + 1)
                nc.scalar.copy(st4[:, :, j, 1:], psr[:, 2 + j % 2, 0:2 * NCH].rearrange("p (q n) -> p q n", q=2)
                               ).then_inc(st_in, 1)
            act.wait_ge(ca_crossed, 16 * 6)
            nc.scalar.copy(ca_re[S:P].rearrange("p j k c -> p (j k c)"), ca_x[S:P]).then_inc(ca_stacked, 1)
            act.wait_ge(pads_set, 1)
            for q in range(NH):
                act.wait_ge(h_mm, q + 1)
                if q >= 2:
                    act.wait_ge(h_out[q % 2], 16 * (q // 2))
                nc.scalar.copy(hbuf[:, q % 2, :, (L - 1) * C:],
                               psr[0:C, q % 4, :].rearrange("p (g m) -> p g m", g=4)).then_inc(h_copied, 1)
            act.wait_ge(st_crossed, 32)
            nc.scalar.copy(st4[S:P, 0, :, 0:NCH], st_x[S:P]).then_inc(st_stacked, 1)
            for y in range(NY):
                gs = y_groups(y)
                act.wait_ge(y_mm, y + 1)
                nc.scalar.activation(z[:, gs[0]:gs[-1] + 1:2, :], psr[:, y % 4, 0:len(gs) * NCH].rearrange(
                    "p (g n) -> p g n", n=NCH), ACT.Gelu_apprx_tanh).then_inc(z_done, 1)

        @block.vector
        def _(dve):
            steps = [0]

            def link(ins):
                ins.then_inc(dve_step, 1)
                steps[0] += 1
                dve.wait_ge(dve_step, steps[0])

            V = nc.vector

            def expm1(x, k, r, e, em, ki):
                link(V.tensor_scalar(x, x, -87.0, 88.0, ALU.max, ALU.min))
                link(V.tensor_scalar(k, x, LOG2E, ROUND, ALU.mult, ALU.add))
                link(V.tensor_scalar(k, k, ROUND, None, ALU.subtract))
                link(V.scalar_tensor_tensor(r, k, -LN2_A, x, ALU.mult, ALU.add))
                link(V.scalar_tensor_tensor(r, k, -LN2_B, r, ALU.mult, ALU.add))
                link(V.tensor_scalar(em, r, FACT[7], None, ALU.mult))
                for n in range(6, 0, -1):
                    link(V.scalar_tensor_tensor(em, em, FACT[n], r, ALU.add, ALU.mult))
                link(V.tensor_scalar(ki, k, 127.0, 8388608.0, ALU.add, ALU.mult))
                two_k = ki.bitcast(F32)
                link(V.scalar_tensor_tensor(e, em, 1.0, two_k, ALU.add, ALU.mult))
                link(V.tensor_tensor(em, em, two_k, ALU.mult))
                link(V.scalar_tensor_tensor(em, two_k, -1.0, em, ALU.add, ALU.add))

            def cmul(o_r, o_i, a_r, a_i, b_r, b_i, m):
                tm_ = ptmp[:, 0:m, :]
                br, bi = (b.unsqueeze(1).to_broadcast([P, m, J]) for b in (b_r, b_i))
                V.tensor_tensor(o_r, a_r, br, ALU.mult)
                link(V.tensor_tensor(tm_, a_i, bi, ALU.mult))
                link(V.tensor_tensor(o_r, o_r, tm_, ALU.subtract))
                V.tensor_tensor(o_i, a_r, bi, ALU.mult)
                link(V.tensor_tensor(tm_, a_i, br, ALU.mult))
                link(V.tensor_tensor(o_i, o_i, tm_, ALU.add))

            R = [lam[:, q, :] for q in range(20)]
            dve.wait_ge(lam_in, 48)
            e_dt = R[19][:, 0:2]
            expm1(ldt[:, :], R[19][:, 2:4], R[19][:, 4:6], e_dt, R[19][:, 6:8], kint[:, 0:2])
            dtb = e_dt.unsqueeze(2).to_broadcast([J, 2, S])
            for q in range(2):
                link(V.tensor_tensor(R[2 + q].rearrange("p (r s) -> p r s", r=2),
                                     R[q].rearrange("p (r s) -> p r s", r=2), dtb, ALU.mult))
            link(V.tensor_scalar(R[4], R[3], 1.0 / (2 * math.pi), ROUND, ALU.mult, ALU.add))
            link(V.tensor_scalar(R[4], R[4], ROUND, None, ALU.subtract))
            link(V.scalar_tensor_tensor(R[5], R[4], -TWO_PI_A, R[3], ALU.mult, ALU.add))
            link(V.scalar_tensor_tensor(R[5], R[4], -TWO_PI_B, R[5], ALU.mult, ALU.add))
            V.tensor_scalar(R[5], R[5], -3.141592, 3.141592, ALU.max, ALU.min).then_inc(angle_ready, 1)
            expm1(R[2], R[4], R[6], R[8], R[9], kint[:, :])
            dve.wait_ge(trig_done, 2)
            link(V.tensor_tensor(R[7], R[10], R[10], ALU.mult))
            link(V.tensor_tensor(R[7], R[7], R[8], ALU.mult))
            link(V.scalar_tensor_tensor(R[16], R[7], -2.0, R[9], ALU.mult, ALU.add))
            link(V.tensor_tensor(R[7], R[10], R[11], ALU.mult))
            link(V.scalar_tensor_tensor(R[13], R[7], 2.0, R[8], ALU.mult, ALU.mult))
            V.tensor_scalar(R[12], R[16], 1.0, None, ALU.add)
            V.tensor_tensor(R[17], R[0], R[0], ALU.mult)
            link(V.tensor_tensor(R[18], R[1], R[1], ALU.mult))
            link(V.tensor_tensor(R[17], R[17], R[18], ALU.add))
            link(V.reciprocal(R[17], R[17]))
            V.tensor_tensor(R[14], R[16], R[0], ALU.mult)
            V.tensor_tensor(R[7], R[13], R[1], ALU.mult)
            V.tensor_tensor(R[15], R[13], R[0], ALU.mult)
            link(V.tensor_tensor(R[18], R[16], R[1], ALU.mult))
            V.tensor_tensor(R[14], R[14], R[7], ALU.add)
            link(V.tensor_tensor(R[15], R[15], R[18], ALU.subtract))
            V.tensor_tensor(R[14], R[14], R[17], ALU.mult)
            V.tensor_tensor(R[15], R[15], R[17], ALU.mult).then_inc(aq_ready, 1)

            dve.wait_ge(gmix_in, 16)
            for i in range(NT):
                n = tile_rows(i)
                dve.wait_ge(rstd_done, i + 1)
                if i >= 2:
                    dve.wait_ge(xt_done, i - 1)
                V.scalar_tensor_tensor(xn[0:n, i % 2, :], xin[0:n, i % 2, :], rstd[0:n, i:i + 1],
                                       gmix[0:n, :], ALU.mult, ALU.mult).then_inc(xn_done, 1)

            dve.wait_ge(aq_t, 1)
            aq = psr[:, 2, 0:4 * J].rearrange("p (q j) -> p q j", q=4)
            V.memset(pw_r[:, 0, :], 1.0)
            V.memset(pw_i[:, 0, :], 0.0)
            V.tensor_copy(pw_r[:, 1, :], aq[:, 0])
            link(V.tensor_copy(pw_i[:, 1, :], aq[:, 1]))
            for m in (1, 2, 4):
                cmul(pw_r[:, m + 1:2 * m + 1], pw_i[:, m + 1:2 * m + 1], pw_r[:, 1:m + 1], pw_i[:, 1:m + 1],
                     pw_r[:, m], pw_i[:, m], m)
            V.tensor_scalar(pw_n[:, :, :], pw_i[:, :, :], -1.0, None, ALU.mult).then_inc(powers_done, 1)
            dve.wait_ge(b_in, 16 * 5)
            qr, qi = (aq[:, 2 + q].unsqueeze(2).to_broadcast([P, J, C]) for q in range(2))
            t1 = tmp[:, :, L, :]
            V.tensor_tensor(bb_re, b_re, qr, ALU.mult)
            link(V.tensor_tensor(t1, b_im, qi, ALU.mult))
            V.tensor_tensor(bb_re, bb_re, t1, ALU.subtract).then_inc(bbar_done, 1)
            dve.wait_ge(bbar_done, 1)
            V.tensor_tensor(bb_im, b_re, qi, ALU.mult)
            link(V.tensor_tensor(t1, b_im, qr, ALU.mult))
            V.tensor_tensor(bb_im, bb_im, t1, ALU.add).then_inc(bbar_done, 1)
            dve.wait_ge(bbar_done, 2)
            V.tensor_copy(pb_r[:, 0], pw_r[:, L])
            link(V.tensor_copy(pb_i[:, 0], pw_i[:, L]))
            for m, n in ((1, 1), (2, 2), (4, 4), (8, BLK - 8)):
                cmul(pb_r[:, m:m + n], pb_i[:, m:m + n], pb_r[:, 0:n], pb_i[:, 0:n],
                     pb_r[:, m - 1], pb_i[:, m - 1], n)
            for q, a, src, sign in ((0, 0, pb_r, 1.0), (0, 1, pb_i, -1.0), (1, 0, pb_i, 1.0), (1, 1, pb_r, 1.0)):
                last = V.tensor_scalar(rot[:, q, a], src.rearrange("p k j -> p j k"), sign, None, ALU.mult)
            link(last)
            dve.wait_ge(c_copied, 2)
            K1 = L + 1

            def over_k(x, k):
                return x.unsqueeze(2).to_broadcast([P, J, k, C])

            def over_c(x, k):
                return x[:, 0:k].rearrange("p k j -> p j k").unsqueeze(3).to_broadcast([P, J, k, C])

            V.tensor_tensor(ca_re[:], over_k(c_re, K1), over_c(pw_r, K1), ALU.mult)
            link(V.tensor_tensor(tmp, over_k(c_im, K1), over_c(pw_i, K1), ALU.mult))
            V.tensor_tensor(ca_re[:], ca_re[:], tmp, ALU.subtract).then_inc(ca_done, 1)
            dve.wait_ge(ca_done, 1)
            dve.wait_ge(ident_step, 2)
            link(V.tensor_tensor(dd, ident[0:C, 0:C].unsqueeze(1).to_broadcast([C, G, C]),
                                 dcol[:, :].unsqueeze(2).to_broadcast([C, G, C]), ALU.mult))

            def ca_ni_step(n):
                js = slice(n // 3 * (J // 8), (n // 3 + 1) * (J // 8))
                shape = [P, J // 8, K1, C]

                def product(dst, c_, pw):
                    return V.tensor_tensor(dst, c_[:, js].unsqueeze(2).to_broadcast(shape),
                                           pw.rearrange("p k j -> p j k")[:, js].unsqueeze(3).to_broadcast(shape),
                                           ALU.mult)

                if n % 3 == 0:
                    product(ca_ni[:, js], c_re, pw_n)
                elif n % 3 == 1:
                    link(product(ca_t, c_im, pw_r))
                else:
                    last = V.tensor_tensor(ca_ni[:, js], ca_ni[:, js], ca_t, ALU.subtract)
                    if n == 23:
                        last.then_inc(ca_done, 1)
                    else:
                        link(last)

            dve.wait_ge(v_prod, L)
            for v, b, sub in ((v_re, bb_im, True), (v_im, bb_re, False)):
                link(V.tensor_tensor(tmp[:, :, 0:L], over_k(b, L), over_c(pw_i, L), ALU.mult))
                V.tensor_tensor(v, v, tmp[:, :, 0:L], ALU.subtract if sub else ALU.add).then_inc(v_done, 1)
                dve.wait_ge(v_done, 1 if sub else 2)
            V.memset(st[:, :, 0:1], 0.0).then_inc(slot0_set, 1)
            for j in range(J):
                dve.wait_ge(vt_mm, j + 1)
                if j >= 2:
                    dve.wait_ge(x_mm, j - 1)
                V.tensor_copy(vt[:, j % 2, :], pst[:, j % 2, 0:2 * P]).then_inc(vt_done, 1)
                if j == 0:
                    dve.wait_ge(ut_out, 16 * DC)
                if 4 <= j < 28:
                    ca_ni_step(j - 4)
            dve.wait_ge(st_in, J)

            def rotate_add(i_rot, src, dst, m):
                pr = reg5[:, 0:4 * J * m].rearrange("p (q a m) -> p q a m", q=2, a=2 * J)
                pr4 = reg5[:, 0:4 * J * m].rearrange("p (q a m) -> p q a m", q=2, a=2)
                sm = reg5[:, 4 * J * m:6 * J * m].rearrange("p (q m) -> p q m", q=2)
                rt = rot[:, :, :, :, i_rot:i_rot + 1].rearrange("p q a j o -> p q (a j) o").to_broadcast([P, 2, 2 * J, m])
                link(V.tensor_tensor(pr, rt, src.unsqueeze(1).to_broadcast([P, 2, 2 * J, m]), ALU.mult))
                link(V.tensor_tensor(sm, pr4[:, :, 0], pr4[:, :, 1], ALU.add))
                link(V.tensor_tensor(dst, dst, sm.rearrange("p q (j m) -> p (q j) m", m=m), ALU.add))

            dve.wait_ge(ca_crossed, 16 * 6)
            for i in range(1, BLK):
                end = (NBLK - 1) * BLK + 1
                rotate_add(0, st[:, :, i:i + end:BLK], st[:, :, 1 + i:1 + i + end:BLK], NBLK)
            for b in range(1, NBLK):
                rotate_add(BLK - 1, st[:, :, b * BLK:b * BLK + 1], st[:, :, (b + 1) * BLK:(b + 1) * BLK + 1], 1)
            V.memset(ptiny[:], 0.0).then_inc(carries_done, 1)
            pr = reg5[:, 0:4 * J * W].rearrange("p (q a i) -> p q a i", q=2, a=2 * J)
            pr4 = reg5[:, 0:4 * J * W].rearrange("p (q a m) -> p q a m", q=2, a=2)
            sm = reg5[:, 4 * J * W:6 * J * W].rearrange("p (q m) -> p q m", q=2)
            for b in range(1, NBLK):
                if b in POOL_BLOCKS:
                    continue
                src = st[:, :, b * BLK:b * BLK + 1].unsqueeze(1).to_broadcast([P, 2, 2 * J, W])
                link(V.tensor_tensor(pr, rot[:, :, :, :, 0:W].rearrange("p q a j i -> p q (a j) i"), src, ALU.mult))
                link(V.tensor_tensor(sm, pr4[:, :, 0], pr4[:, :, 1], ALU.add))
                dst = st[:, :, 1 + b * BLK:1 + b * BLK + W]
                link(V.tensor_tensor(dst, dst, sm.rearrange("p q (j i) -> p (q j) i", i=W), ALU.add))
            V.memset(ptiny[:], 0.0).then_inc(st_done, 1)
            dve.wait_ge(st_crossed, 32)
            V.tensor_copy(st4[0:S, 1, :, 0:NCH], st_x[0:S]).then_inc(st_stacked, 1)

        @block.tensor
        def _(pe):
            T = nc.tensor
            pe.wait_ge(ident_step, 2)
            pe.wait_ge(c_in, 16 * 16)
            for part in range(2):
                for q in range(4):
                    last = T.transpose(psr[:, part, q * P:(q + 1) * P], c_raw[:, part, q, :], ident[:])
            last.then_inc(ct_done, 1)
            pe.wait_ge(aq_ready, 1)
            for q in range(4):
                last = T.transpose(psr[:, 2, q * J:(q + 1) * J], lam[:, 12 + q, :], ident[0:J, 0:J])
            last.then_inc(aq_t, 1)
            for i in range(NT):
                n = tile_rows(i)
                pe.wait_ge(xn_done, i + 1)
                if i >= 2:
                    pe.wait_ge(ut_done, 2 * (i - 1))
                for c in range(DC):
                    last = T.transpose(pst[:, i % 2, c * P:c * P + n], xn[0:n, i % 2, c * P:(c + 1) * P],
                                       ident[0:n, 0:n])
                last.then_inc(xt_done, 1)
            pe.wait_ge(v_done, 2)
            pe.wait_ge(ut_done, 2 * NT)
            pe.wait_ge(uc_in, 16 * L)
            for j in range(J + 1):
                if j < J:
                    if j >= 2:
                        pe.wait_ge(vt_done, j - 1)
                    for q, v in enumerate((v_re, v_im)):
                        last = T.transpose(pst[:, j % 2, q * P:(q + 1) * P],
                                           v[:, j].rearrange("p k c -> p (k c)"), ident[:])
                    last.then_inc(vt_mm, 1)
                if j >= 1:
                    i = j - 1
                    pe.wait_ge(vt_done, i + 1)
                    if i >= 2:
                        pe.wait_ge(st_in, i - 1)
                    for r in range(2):
                        for q in range(2):
                            last = T.matmul(psr[r * S:(r + 1) * S, 2 + i % 2, q * NCH:(q + 1) * NCH],
                                            vt[:, i % 2, q * P + r * S:q * P + (r + 1) * S],
                                            uc[:, 2 * i + r, :], start=True, stop=True)
                    last.then_inc(x_mm, 1)
            pe.wait_ge(ca_stacked, 2)
            pe.wait_ge(c_copied, 2)
            pe.wait_ge(st_in, J)
            for q in range(NH):
                if q >= 4:
                    pe.wait_ge(h_copied, q - 3)
                r = q % 2
                for gi in range(4):
                    j = 4 * (q // 2) + gi
                    T.matmul(psr[0:C, q % 4, gi * P:(gi + 1) * P], bb_st[:, r, j, :],
                             (ca_re, ca_ni)[r][:, j, 0:L, :].rearrange("p k c -> p (k c)"),
                             start=True, stop=False)
                    last = T.matmul(psr[0:C, q % 4, gi * P:gi * P + C], ident[0:C, 0:C], dd[:, 2 * j + r, :],
                                    start=False, stop=True)
                last.then_inc(h_mm, 1)
            pe.wait_ge(tm_in, 16 * L)
            pe.wait_ge(st_stacked, 2)
            for y in range(NY):
                if y >= 4:
                    pe.wait_ge(z_done, y - 3)
                for k, g in enumerate(y_groups(y)):
                    r, j = g % 2, g // 2
                    out = psr[:, y % 4, k * NCH:(k + 1) * NCH]
                    T.matmul(out, tm[:, g, :], uc[:, g, :], start=True, stop=False)
                    last = T.matmul(out, (ca_re, ca_ni)[r][:, j, 1:, :].rearrange("p k c -> p (k c)"),
                                    st4[:, r, j, 0:NCH], start=False, stop=True)
                last.then_inc(y_mm, 1)


def phase_glu(nc, t):
    NT = XT + 1
    NQ = 4
    QW = D // NQ
    BANKS = 6
    h, z_dram = t["h"], t["z_dram"]
    w_glu = t["ssm_w_glu"][0].rearrange("(p c) (v q m) -> p c v q m", c=DC, v=2, q=NQ)
    with ExitStack() as ctx:
        def sb(name, shape, dt=F32):
            return ctx.enter_context(nc.sbuf_tensor("glu_" + name, shape, dt))

        sem = semaphore_source(nc, ctx, "glu_")

        z_raw = sb("z_raw", [P, 2, L, NCH])
        z_hi, z_lo = (sb(f"z_{x}", [P, DC, T_ALL], F32R) for x in ("hi", "lo"))
        w_raw = sb("w_raw", [P, 2, DC // 2, 2, QW])
        w_hi, w_lo = (sb(f"w_{x}", [P, 2, DC, 2 * QW], F32R) for x in ("hi", "lo"))
        sig = sb("sig", [P, 2, QW])
        val = sb("val", [P, 2, QW])
        acc = ctx.enter_context(nc.psum_tensor("glu_acc", [P, BANKS, 512], F32))

        z_in = [sem(f"z_in{b}") for b in range(2)]
        w_in = [sem(f"w_in{b}") for b in range(2)]
        h_in, z_hi_done, z_lo_done, w_hi_done, w_lo_done = (
            sem(x) for x in ("h_in", "z_hi_done", "z_lo_done", "w_hi_done", "w_lo_done"))
        acc_done, sig_done, val_done, h_done = (sem(x) for x in ("acc_done", "sig_done", "val_done", "h_done"))
        block = ctx.enter_context(nc.Block())

        @block.sync
        def _(sp):
            z_pc = z_dram.rearrange("(p c) s n -> p c s n", c=DC)

            def load_w(q, half):
                sp.dma_start(w_raw[:, half], w_glu[:, 4 * half:4 * half + 4, :, q, :]).then_inc(w_in[half], 16)

            for c in range(DC):
                if c >= 2:
                    sp.wait_ge(z_lo_done, c - 1)
                sp.dma_start(z_raw[:, c % 2], z_pc[:, c]).then_inc(z_in[c % 2], 16)
                if c == 1:
                    for half in range(2):
                        load_w(0, half)
            for i in range(NT):
                n = tile_rows(i)
                src = t["x"][0, i * P:(i + 1) * P, :] if i < XT else t["meta_tokens"]
                sp.dma_start(h[0:n, i, :], src).then_inc(h_in, 16)
            for q in range(1, NQ):
                for half in range(2):
                    sp.wait_ge(w_lo_done, 2 * (q - 1) + half + 1)
                    load_w(q, half)

        @block.scalar
        def _(act):
            def split_w(q):
                for half in range(2):
                    act.wait_ge(w_in[half], 16 * (q + 1))
                    if q >= 2:
                        act.wait_ge(acc_done, NT * (q - 1))
                    nc.scalar.copy(w_hi[:, q % 2, 4 * half:4 * half + 4, :],
                                   w_raw[:, half].rearrange("p c v m -> p c (v m)")).then_inc(w_hi_done, 1)

            for c in range(DC):
                act.wait_ge(z_in[c % 2], 16 * (c // 2 + 1))
                nc.scalar.copy(z_hi[:, c, :].rearrange("p (n s) -> p n s", s=L),
                               z_raw[:, c % 2].rearrange("p s n -> p n s")).then_inc(z_hi_done, 1)
                if c == 1:
                    split_w(0)
            for q in range(NQ):
                if q + 1 < NQ:
                    split_w(q + 1)
                for i in range(NT):
                    k, n = q * NT + i, tile_rows(i)
                    act.wait_ge(acc_done, k + 1)
                    if k >= 2:
                        act.wait_ge(val_done, k - 1)
                    nc.scalar.activation(sig[0:n, k % 2, :], acc[0:n, k % BANKS, QW:2 * QW],
                                         ACT.Sigmoid).then_inc(sig_done, 1)

        @block.vector
        def _(dve):
            V = nc.vector

            def split_w(q):
                for half in range(2):
                    dve.wait_ge(w_hi_done, 2 * q + half + 1)
                    cs = slice(4 * half, 4 * half + 4)
                    V.tensor_tensor(w_lo[:, q % 2, cs, :], w_raw[:, half].rearrange("p c v m -> p c (v m)"),
                                    w_hi[:, q % 2, cs, :].bitcast(F32), ALU.subtract).then_inc(w_lo_done, 1)

            for c in range(DC):
                dve.wait_ge(z_hi_done, c + 1)
                V.tensor_tensor(z_lo[:, c, :].rearrange("p (n s) -> p n s", s=L),
                                z_raw[:, c % 2].rearrange("p s n -> p n s"),
                                z_hi[:, c, :].bitcast(F32).rearrange("p (n s) -> p n s", s=L),
                                ALU.subtract).then_inc(z_lo_done, 1)
                if c == 1:
                    split_w(0)
            dve.wait_ge(h_in, 16 * NT)
            for q in range(NQ):
                if q + 1 < NQ:
                    split_w(q + 1)
                for i in range(NT):
                    k, n = q * NT + i, tile_rows(i)
                    dve.wait_ge(sig_done, k + 1)
                    if k >= 2:
                        dve.wait_ge(h_done, k - 1)
                    V.tensor_tensor(val[0:n, k % 2, :], acc[0:n, k % BANKS, 0:QW], sig[0:n, k % 2, :],
                                    ALU.mult).then_inc(val_done, 1)
                    dve.wait_ge(val_done, k + 1)
                    hq = h[0:n, i, q * QW:(q + 1) * QW]
                    V.tensor_tensor(hq, hq, val[0:n, k % 2, :], ALU.add).then_inc(h_done, 1)

        @block.tensor
        def _(pe):
            def products(q, i, c):
                n = tile_rows(i)
                pos = N_META + i * P if i < XT else 0
                out = acc[0:n, (q * NT + i) % BANKS, :]
                zh, zl = z_hi[:, c, pos:pos + n], z_lo[:, c, pos:pos + n]
                wh, wl = w_hi[:, q % 2, c, :], w_lo[:, q % 2, c, :]
                nc.tensor.matmul(out, zh, wh, start=(c == 0), stop=False)
                nc.tensor.matmul(out, zl, wh, start=False, stop=False)
                return nc.tensor.matmul(out, zh, wl, start=False, stop=(c == DC - 1))

            for c in range(DC):
                pe.wait_ge(z_lo_done, c + 1)
                pe.wait_ge(w_lo_done, 2 * c // DC + 1)
                for i in range(BANKS):
                    last = products(0, i, c)
                    if c == DC - 1:
                        last.then_inc(acc_done, 1)
            for q in range(NQ):
                pe.wait_ge(w_lo_done, 2 * (q + 1))
                for i in range(BANKS if q == 0 else 0, NT):
                    k = q * NT + i
                    if k >= BANKS:
                        pe.wait_ge(val_done, k - BANKS + 1)
                    for c in range(DC):
                        last = products(q, i, c)
                    last.then_inc(acc_done, 1)


N_GRP = 4
E_GRP = 8
N_EXP = N_GRP * E_GRP
F = D // 2
FC = F // P
RT = -(-T_ALL // P)
NO_TOKEN = 8192


def phase_moe(nc, t, layer, out=None):
    NT = XT + 1 if layer == 0 else XT
    last_layer = out is not None
    KC = DC // 2
    FW = FC // 2
    COLS = RT * N_EXP
    ROWS = SEQ + (N_META if layer == 0 else 0)
    XB = 3
    NB = 6
    h = t["h"]
    xn_dram, y_dram = t[f"xn_dram{layer}"], t[f"y_dram{layer}"]
    w_gate = t["moe_w_gate"][layer].rearrange("e (p c) f -> e p c f", c=DC)
    w_up = t["moe_w_up"][layer].rearrange("e (p c) f -> e p c f", c=DC)
    w_down = t["moe_w_down"][layer].rearrange("e (p c) d -> e p c d", c=FC)
    with ExitStack() as ctx:
        def sb(name, shape, dt=F32):
            return ctx.enter_context(nc.sbuf_tensor(f"moe{layer}_{name}", shape, dt))

        def ps(name, banks):
            return ctx.enter_context(nc.psum_tensor(f"moe{layer}_{name}", [P, banks * 512], F32))

        sem = semaphore_source(nc, ctx, f"moe{layer}_")

        ident = sb("ident", [P, P])
        ones = sb("ones", [P, P])
        tri = sb("tri", [P, P])
        mhalf = sb("mhalf", [P, 1])
        work = sb("work", [P, 6 * D])
        xn = work[:, 0:XB * D].rearrange("p (b d) -> p b d", b=XB)
        gain = work[:, 3 * D:4 * D]
        xt_r = work[:, 4 * D:6 * D].rearrange("p (b c m) -> p b c m", b=2, c=DC)
        vk = work[:, 0:2 * NT * COLS].rearrange("p (k i r e) -> p k i r e", k=2, i=NT, e=N_EXP)
        w_rt = sb("w_rt", [P, DC, N_GRP + N_EXP])
        b_rt = sb("b_rt", [P, N_GRP + N_EXP])
        lg = sb("lg", [P, NT, N_GRP + N_EXP])
        ss = sb("ss", [P, NT])
        rstd = sb("rstd", [P, NT])
        col = {x: sb(x, [P, NT]) for x in ("gmax", "mw", "pg", "m1", "m2", "e2", "pos", "rt", "tmpc", "jpos1", "jpos2")}
        gates = sb("gates", [P, 2, NT])
        w4, ohg, eg = (sb(x, [P, NT, N_GRP]) for x in ("w4", "ohg", "eg"))
        w8, sel, oh1, oh2 = (sb(x, [P, NT, E_GRP]) for x in ("w8", "sel", "oh1", "oh2"))
        big = sb("big", [P, NT, N_EXP])
        msk = sb("msk", [P, 2, NT, N_EXP])
        msum = sb("msum", [P, NT, N_EXP])
        pfx = sb("pfx", [P, NT, N_EXP])
        cum = sb("cum", [P, NT, N_EXP])
        ge = sb("ge", [P, NT, RT - 1])
        ohr = sb("ohr", [P, NT, RT])
        oh_slot = sb("oh_slot", [P, 4, P])
        iota_i = sb("iota_i", [P, COLS], I32)
        iota_p1 = sb("iota_p1", [P, 1])
        desc = sb("desc", [P, E_GRP])
        thr = sb("thr", [P, RT - 1])
        iota_r = sb("iota_r", [P, RT])
        iota_m = sb("iota_m", [P, P])
        iota_c = sb("iota_c", [P, COLS])
        code = sb("code", [P, 2, NT])
        act_f = sb("act_f", [P, COLS - N_EXP])
        act_p = sb("act_p", [P, COLS - N_EXP])
        act_o = sb("act_o", [P, COLS - N_EXP])
        ones_r = sb("ones_r", [P, COLS - N_EXP])
        over = sb("over", [P, 2])
        slot_f = sb("slot_f", [P, COLS])
        idx_out = sb("idx_out", [P, COLS], I32)
        idx_in = sb("idx_in", [P, COLS], I32)
        tile_col = sb("tile_col", [1, 2 * N_EXP], I32)
        tile_exp = sb("tile_exp", [1, 2 * N_EXP], I32)
        n_more = sb("n_more", [1, 1], I32)
        raw = sb("raw", [P, 6, KC * F])
        hi, lo = (sb(x, [P, 3, KC * F], F32R) for x in ("hi", "lo"))
        gi = sb("gi", [P, 1], I32)
        unit = sb("unit", [P, 2])
        si = sb("si", [P, 1], I32)
        xg = sb("xg", [P, D])
        x_hi, x_lo = (sb(f"x_{x}", [P, DC, P], F32R) for x in ("hi", "lo"))
        silu = sb("silu", [P, F])
        hid = sb("hid", [P, F])
        h_hi, h_lo = (sb(f"h_{x}", [P, FC, P], F32R) for x in ("hi", "lo"))
        y = sb("y", [P, D])

        ps_g, ps_u, ps_ht, ps_m = ps("ps_g", 1), ps("ps_u", 1), ps("ps_ht", 1), ps("ps_m", 1)
        ps_y, ps_xt = ps("ps_y", 2), ps("ps_xt", 2)
        ps_r = (ps_xt, ps_y)

        ident_step, consts_set, rt_in, b_rt_in, gain_in, squares_done, pool_step, rstd_done, xn_done = (
            sem(x) for x in ("ident_step", "consts_set", "rt_in", "b_rt_in", "gain_in", "squares_done",
                             "pool_step", "rstd_done", "xn_done"))
        xn_out = [sem(f"xn_out{b}") for b in range(XB)]
        xt_mm_r, xt_cp_r, lg_mm, lg_done, exp_ready, exp_done, dve_step, mask_ready, pfx_mm = (
            sem(x) for x in ("xt_mm_r", "xt_cp_r", "lg_mm", "lg_done", "exp_ready", "exp_done", "dve_step",
                             "mask_ready", "pfx_mm"))
        iotas_set, oh_done, slot_mm, over_ready, over_t, list_ready = (
            sem(x) for x in ("iotas_set", "oh_done", "slot_mm", "over_ready", "over_t", "list_ready"))
        raw_in = [sem(f"raw_in{k}") for k in range(6)]
        hi_done, lo_done, w_used = (sem(x) for x in ("hi_done", "lo_done", "w_used"))
        ix_step, xg_in, xt_mm, xt_hi, xt_lo, silu_done, hid_done, ht_mm, ht_hi, ht_lo, y_done, y_out = (
            sem(x) for x in ("ix_step", "xg_in", "xt_mm", "xt_hi", "xt_lo", "silu_done", "hid_done",
                             "ht_mm", "ht_hi", "ht_lo", "y_done", "y_out"))
        yc_in = [sem(f"yc_in{b}") for b in range(NB)]
        y_free, h_new, fin_sq, fin_rstd, fin_done, out_done = (
            sem(x) for x in ("y_free", "h_new", "fin_sq", "fin_rstd", "fin_done", "out_done"))
        yc = raw[:, :, :].rearrange("p k (c d) -> p k c d", c=2)

        def first_pieces(k):
            return 2 + k

        block = ctx.enter_context(nc.Block())

        @block.sync
        def _(sp):
            def load(k, expert):
                if k < 4:
                    src = (w_gate, w_up)[k // 2][expert][:, KC * (k % 2):KC * (k % 2 + 1), :]
                else:
                    src = w_down[expert][:, FW * (k - 4):FW * (k - 3), :]
                sp.dma_start(raw[:, k, :].rearrange("p (c f) -> p c f", c=KC if k < 4 else FW),
                             src).then_inc(raw_in[k], 16)

            sp.dma_start(gain, t["norm_ffn"][layer].partition_broadcast(P)).then_inc(gain_in, 16)
            sp.dma_start(w_rt[:, :, 0:N_GRP],
                         t["moe_w_grp"][layer].rearrange("(p c) n -> p c n", c=DC)).then_inc(rt_in, 16)
            sp.dma_start(w_rt[:, :, N_GRP:],
                         t["moe_w_exp"][layer].rearrange("(p c) n -> p c n", c=DC)).then_inc(rt_in, 16)
            sp.dma_start(b_rt[:, 0:N_GRP], t["moe_b_grp"][layer].partition_broadcast(P)).then_inc(b_rt_in, 16)
            sp.dma_start(b_rt[:, N_GRP:], t["moe_b_exp"][layer].partition_broadcast(P)).then_inc(b_rt_in, 16)
            for i in range(NT):
                sp.wait_ge(xn_done, i + 1)
                sp.dma_start(xn_dram[i * P:i * P + tile_rows(i), :], xn[0:tile_rows(i), i % XB, :]).then_inc(xn_out[i % XB], 16)
                if i < NB:
                    load(i, 0)
            for k in range(4):
                sp.wait_ge(lo_done, first_pieces(k) + 1)
                load(k, 1)
            sp.wait_ge(list_ready, 1)
            n_q = sp.value_load(n_more[0:1, 0:1], min_val=0, max_val=N_EXP) + N_EXP

            def load_of(k, tile, number):
                expert = sp.value_load(tile_exp[0:1, bass.ds(tile, 1)], min_val=0, max_val=N_EXP - 1)
                for i, kk in enumerate(k):
                    sp.wait_ge(lo_done, number + (i - NB + 1))
                    sp.wait_ge(list_ready, 1)
                    src_e = bass.ds(expert, 1)
                    if kk < 4:
                        src = (w_gate, w_up)[kk // 2][src_e][:, :, KC * (kk % 2):KC * (kk % 2 + 1), :]
                    else:
                        src = w_down[src_e][:, :, FW * (kk - 4):FW * (kk - 3), :]
                    sp.dma_start(raw[:, kk, :].rearrange("p (c f) -> p c f", c=KC if kk < 4 else FW),
                                 src.rearrange("o p c f -> (o p) c f")).then_inc(raw_in[kk], 16)

            with sp.Fori(2, n_q) as e:
                load_of(range(4), e, e * 6)
                load_of(range(4, 6), e - 1, e * 6 + 4)
            load_of(range(4, 6), n_q - 1, n_q * 6 + 4)
            if last_layer:
                sp.dma_start(gain, t["norm_final"].partition_broadcast(P)).then_inc(gain_in, 16)
            sp.wait_ge(y_free, n_q + 1)
            for i in range(NT):
                if i >= NB:
                    sp.wait_ge(h_new, 2 * (i - NB + 1))
                sp.dma_start(yc[0:tile_rows(i), i % NB],
                             y_dram[2 * i * P:2 * (i * P + tile_rows(i)), :].rearrange("(p k) d -> p k d", k=2)
                             ).then_inc(yc_in[i % NB], 16)
            if last_layer:
                for i in range(NT):
                    sp.wait_ge(fin_done, i + 1)
                    sp.dma_start(out[0, i * P:(i + 1) * P, :], h[:, i, :]).then_inc(out_done, 16)
                sp.wait_ge(out_done, 16 * NT)
            for b in range(XB):
                sp.wait_ge(xn_out[b], 16 * ((NT + XB - 1 - b) // XB))

        @block.gpsimd
        def _(pool):
            G_ = nc.gpsimd
            G_.memset(y[:, 0:1], 0.0).then_inc(y_free, 1)
            G_.memset(mhalf[:], -0.5).then_inc(consts_set, 1)
            make_identity(nc, pool, ident, ident_step)
            G_.memset(ones[:], 1.0).then_inc(consts_set, 1)
            G_.memset(ones_r[:], 1.0).then_inc(consts_set, 1)
            pool.wait_ge(consts_set, 2)
            G_.affine_select(out=tri[:], in_=ones[:], compare_op=ALU.is_gt, fill=0.0, base=0,
                             pattern=[[1, P]], channel_multiplier=-1).then_inc(consts_set, 1)
            n_pool = [0]

            def link(ins):
                ins.then_inc(pool_step, 1)
                n_pool[0] += 1
                pool.wait_ge(pool_step, n_pool[0])

            def iota(dst, pattern, base, mult):
                n = int(np.prod([c for _, c in pattern]))
                link(G_.iota(iota_i[:, 0:n], pattern=pattern, base=base, channel_multiplier=mult))
                link(G_.tensor_copy(dst, iota_i[:, 0:n]))

            def iotas():
                iota(iota_p1[:, :], [[0, 1]], 1, 1)
                iota(desc[:, :], [[-1, E_GRP]], E_GRP, 0)
                iota(thr[:, :], [[P, RT - 1]], P, 0)
                iota(iota_r[:, :], [[1, RT]], 0, 0)
                iota(iota_m[:, :], [[1, P]], 0, 0)
                iota(iota_c[:, :], [[1, COLS]], 0, 0)
                for k in range(2):
                    iota(code[:, k, :], [[2 * P, NT]], 1 + k, 2)
                link(G_.iota(tile_col[:, 0:N_EXP], pattern=[[1, N_EXP]], base=0, channel_multiplier=0))
                link(G_.iota(tile_exp[:, 0:N_EXP], pattern=[[1, N_EXP]], base=0, channel_multiplier=0))
                G_.memset(unit[:], 0.0).then_inc(iotas_set, 1)

            for i in range(NT):
                pool.wait_ge(squares_done, i + 1)
                s_i, r_i = ss[0:tile_rows(i), i:i + 1], rstd[0:tile_rows(i), i:i + 1]
                link(G_.tensor_scalar(s_i, s_i, 1.0 / D, EPS, ALU.mult, ALU.add))
                G_.tensor_tensor(r_i, s_i, mhalf[0:tile_rows(i), :], ALU.pow).then_inc(rstd_done, 1)
                if i == XB:
                    iotas()

            for k in range(3):
                n = first_pieces(k)
                pool.wait_ge(hi_done, n + 1)
                G_.tensor_tensor(lo[:, n % 3, :], raw[:, k, :], hi[:, n % 3, :].bitcast(F32),
                                 ALU.subtract).then_inc(lo_done, 3 if k == 0 else 1)

            pool.wait_ge(list_ready, 1)
            for b in range(XB):
                pool.wait_ge(xn_out[b], 16 * ((NT + XB - 1 - b) // XB))
            n_q = pool.value_load(n_more[0:1, 0:1], min_val=0, max_val=N_EXP) + N_EXP
            pool.wait_ge(iotas_set, 1)

            def column(dst, idx, tile, step):
                pool.wait_ge(list_ready, 1)
                c = pool.value_load(tile_col[0:1, bass.ds(tile, 1)], min_val=0, max_val=COLS - 1)
                G_.tensor_copy(dst[:, :], idx[:, bass.ds(c, 1)]).then_inc(ix_step, 1)
                pool.wait_ge(ix_step, step)
                G_.tensor_tensor(unit[:, 0:1], mhalf[:, :], mhalf[:, :], ALU.mult)

            last_x, last_y = pool.to_reg(ROWS - 1), pool.to_reg(2 * ROWS - 1)

            def gather(tile, step):
                column(gi, idx_in, tile, step)
                G_.indirect_dma_start(xg[:, :], None, xn_dram[:, :],
                                      bass.IndirectOffsetOnAxis(gi[:, :].bitcast(U32), 0),
                                      bounds_check=last_x, oob_is_err=False).then_inc(xg_in, 16)

            def scatter(tile, step):
                column(si, idx_out, tile, step)
                G_.indirect_dma_start(y_dram[:, :], bass.IndirectOffsetOnAxis(si[:, :].bitcast(U32), 0),
                                      y[:, :], None,
                                      bounds_check=last_y, oob_is_err=False).then_inc(y_out, 16)
                pool.wait_ge(y_out, tile * 16 + 16)
                G_.tensor_tensor(unit[:, 1:2], mhalf[:, :], mhalf[:, :], ALU.mult).then_inc(y_free, 1)

            gather(0, 1)
            for tile in range(1, 3):
                pool.wait_ge(xt_mm, tile)
                gather(tile, tile + 1)
            with pool.Fori(1, n_q - 2) as e:
                pool.wait_ge(xt_mm, e + 2)
                gather(e + 2, e * 2 + 2)
                pool.wait_ge(y_done, e)
                scatter(e - 1, e * 2 + 3)
            for last in range(3):
                pool.wait_ge(y_done, n_q + (last - 2))
                scatter(n_q + (last - 3), n_q * 2 + (last - 2))
            if last_layer:
                for i in range(NT):
                    pool.wait_ge(fin_sq, i + 1)
                    s_i, r_i = ss[:, i:i + 1], rstd[:, i:i + 1]
                    link(G_.tensor_scalar(s_i, s_i, 1.0 / D, EPS, ALU.mult, ALU.add))
                    G_.tensor_tensor(r_i, s_i, mhalf[:, :], ALU.pow).then_inc(fin_rstd, 1)

        @block.scalar
        def _(act):
            A = nc.scalar

            def squares(i):
                if i:
                    act.wait_ge(squares_done, i)
                A.activation(xg[0:tile_rows(i)], h[0:tile_rows(i), i, :], ACT.Square,
                             accum_out=ss[0:tile_rows(i), i:i + 1]).then_inc(squares_done, 1)

            squares(0)
            for i in range(NT):
                if i + 1 < NT:
                    squares(i + 1)
                act.wait_ge(xt_mm_r, i + 1)
                if i >= 2:
                    act.wait_ge(lg_mm, i - 1)
                n = tile_rows(i)
                A.copy(xt_r[:, i % 2, :, 0:n],
                       ps_r[i % 2].rearrange("p (c m) -> p c m", c=DC)[:, :, 0:n]).then_inc(xt_cp_r, 1)
            act.wait_ge(exp_ready, 1)
            A.activation(eg[:, :, :], eg[:, :, :], ACT.Exp).then_inc(exp_done, 1)
            act.wait_ge(exp_ready, 2)
            A.activation(col["e2"][:, :], col["e2"][:, :], ACT.Exp).then_inc(exp_done, 1)
            for k in range(3):
                act.wait_ge(raw_in[k], 16)
                A.copy(hi[:, first_pieces(k) % 3, :], raw[:, k, :]).then_inc(hi_done, 3 if k == 0 else 1)
            act.wait_ge(list_ready, 1)
            n_q = act.value_load(n_more[0:1, 0:1], min_val=0, max_val=N_EXP) + N_EXP

            def split_hi(number, k, loads):
                act.wait_ge(raw_in[k], loads)
                act.wait_ge(w_used, number - 2)
                A.copy(hi[:, slot(number, k), :], raw[:, k, :]).then_inc(hi_done, 1)

            def slot(number, k):
                return number % 3 if isinstance(number, int) else k % 3

            def x_hi_part(e):
                act.wait_ge(xt_mm, e + 1)
                A.copy(x_hi[:, :, :].rearrange("p c m -> p (c m)"), ps_xt[:, :]).then_inc(xt_hi, 1)

            def silu_of(e):
                act.wait_ge(w_used, 4 if isinstance(e, int) and e == 0 else e * 6 + 2)
                A.activation(silu[:, :], ps_g[:, :], ACT.Silu).then_inc(silu_done, 1)

            def hidden_hi_part(e):
                act.wait_ge(ht_mm, e + 1)
                A.copy(h_hi[:, :, :].rearrange("p c m -> p (c m)"), ps_ht[:, :]).then_inc(ht_hi, 1)

            def store_y(e, used):
                act.wait_ge(w_used, used)
                act.wait_ge(y_free, e + 1)
                A.copy(y[:, :], ps_y[:, :]).then_inc(y_done, 1)

            x_hi_part(0)
            split_hi(first_pieces(3), 3, 16)
            silu_of(0)
            x_hi_part(1)
            for k in range(3):
                split_hi(6 + k, k, 32)
            hidden_hi_part(0)
            with act.Fori(1, n_q - 1) as e:
                split_hi(e * 6 + 3, 3, e * 16 + 16)
                split_hi(e * 6 + 4, 4, e * 16)
                act.wait_ge(hid_done, e)
                silu_of(e)
                split_hi(e * 6 + 5, 5, e * 16)
                x_hi_part(e + 1)
                for k in range(3):
                    split_hi(e * 6 + 6 + k, k, e * 16 + 32)
                hidden_hi_part(e)
                store_y(e - 1, e * 6 + 6)
            split_hi(n_q * 6 - 3, 3, n_q * 16)
            split_hi(n_q * 6 - 2, 4, n_q * 16 - 16)
            act.wait_ge(hid_done, n_q - 1)
            silu_of(n_q - 1)
            split_hi(n_q * 6 - 1, 5, n_q * 16 - 16)
            for k in range(2):
                act.wait_ge(raw_in[4 + k], n_q * 16)
                act.wait_ge(w_used, n_q * 6 + k - 2)
                A.copy(hi[:, k, :], raw[:, 4 + k, :]).then_inc(hi_done, 1)
            hidden_hi_part(n_q - 1)
            store_y(n_q - 2, n_q * 6)
            store_y(n_q - 1, n_q * 6 + 2)
            if last_layer:
                for i in range(NT):
                    act.wait_ge(h_new, 2 * (i + 1))
                    if i:
                        act.wait_ge(fin_sq, i)
                    A.activation(xg[:, :], h[:, i, :], ACT.Square, accum_out=ss[:, i:i + 1]).then_inc(fin_sq, 1)

        @block.vector
        def _(dve):
            V = nc.vector
            n_dve = [0]

            def link(ins):
                ins.then_inc(dve_step, 1)
                n_dve[0] += 1
                dve.wait_ge(dve_step, n_dve[0])

            if NT > XT:
                link(V.memset(lg[:, XT, :], 0.0))
            dve.wait_ge(gain_in, 16)
            dve.wait_ge(b_rt_in, 32)

            def logits(i):
                dve.wait_ge(lg_mm, i + 1)
                V.tensor_tensor(lg[0:tile_rows(i), i, :], ps_m[0:tile_rows(i), 0:N_GRP + N_EXP], b_rt[0:tile_rows(i), :],
                                ALU.add).then_inc(lg_done, 1)

            for i in range(NT):
                n = tile_rows(i)
                dve.wait_ge(rstd_done, i + 1)
                if i >= XB:
                    dve.wait_ge(xt_mm_r, i - XB + 1)
                    dve.wait_ge(xn_out[i % XB], 16 * (i // XB))
                V.scalar_tensor_tensor(xn[0:n, i % XB, :], h[0:n, i, :], rstd[0:n, i:i + 1], gain[0:n, :],
                                       ALU.mult, ALU.mult).then_inc(xn_done, 1)
                if i >= 2:
                    logits(i - 2)
            logits(NT - 2)
            logits(NT - 1)
            dve.wait_ge(lg_done, NT)
            dve.wait_ge(iotas_set, 1)

            def over_last(x, n):
                return x.unsqueeze(2).to_broadcast([P, NT, n])

            def first_max(values, n, top, weights, onehot):
                link(V.reduce_max(top, values, AX.X))
                link(V.tensor_tensor(weights, values, over_last(top, n), ALU.is_equal))
                link(V.tensor_tensor(weights, weights,
                                     desc[:, E_GRP - n:].unsqueeze(1).to_broadcast([P, NT, n]), ALU.mult))
                link(V.reduce_max(col["mw"][:, :], weights, AX.X))
                link(V.tensor_tensor(onehot, weights, over_last(col["mw"][:, :], n), ALU.is_equal))

            lg_g = lg[:, :, 0:N_GRP]
            first_max(lg_g, N_GRP, col["gmax"][:, :], w4[:, :, :], ohg[:, :, :])
            V.tensor_tensor(eg[:, :, :], lg_g, over_last(col["gmax"][:, :], N_GRP), ALU.subtract).then_inc(exp_ready, 1)
            big4 = big[:, :, :].rearrange("p i (g e) -> p i g e", g=N_GRP)
            link(V.tensor_tensor(big4, lg[:, :, N_GRP:].rearrange("p i (g e) -> p i g e", g=N_GRP),
                                 ohg[:, :, :].unsqueeze(3).to_broadcast([P, NT, N_GRP, E_GRP]), ALU.mult))
            link(V.tensor_reduce(sel[:, :, :], big4.rearrange("p i g e -> p i e g"), AX.X, ALU.add))
            first_max(sel[:, :, :], E_GRP, col["m1"][:, :], w8[:, :, :], oh1[:, :, :])
            link(V.scalar_tensor_tensor(sel[:, :, :], oh1[:, :, :], -1e30, sel[:, :, :], ALU.mult, ALU.add))
            first_max(sel[:, :, :], E_GRP, col["m2"][:, :], w8[:, :, :], oh2[:, :, :])
            V.tensor_tensor(col["e2"][:, :], col["m2"][:, :], col["m1"][:, :], ALU.subtract).then_inc(exp_ready, 1)
            if NT > XT:
                link(V.tensor_scalar(col["tmpc"][:, 0:1], iota_p1[:, :], float(N_META), None, ALU.is_le))
                link(V.tensor_scalar(ohg[:, XT, :], ohg[:, XT, :], col["tmpc"][:, 0:1], None, ALU.mult))
            g_b = ohg[:, :, :].unsqueeze(3).to_broadcast([P, NT, N_GRP, E_GRP])
            for k, oh in enumerate((oh1, oh2)):
                link(V.tensor_tensor(msk[:, k].rearrange("p i (g e) -> p i g e", g=N_GRP), g_b,
                                     oh[:, :, :].unsqueeze(2).to_broadcast([P, NT, N_GRP, E_GRP]), ALU.mult))
            V.tensor_tensor(msum[:, :, :], msk[:, 0], msk[:, 1], ALU.add).then_inc(mask_ready, 1)
            dve.wait_ge(exp_done, 2)
            link(V.reduce_sum(col["pg"][:, :], eg[:, :, :], AX.X))
            link(V.reciprocal(col["pg"][:, :], col["pg"][:, :]))
            link(V.tensor_scalar(col["tmpc"][:, :], col["e2"][:, :], 1.0, None, ALU.add))
            link(V.reciprocal(col["tmpc"][:, :], col["tmpc"][:, :]))
            link(V.tensor_tensor(gates[:, 0, :], col["pg"][:, :], col["tmpc"][:, :], ALU.mult))
            link(V.tensor_tensor(gates[:, 1, :], gates[:, 0, :], col["e2"][:, :], ALU.mult))
            dve.wait_ge(pfx_mm, 1)
            link(V.tensor_copy(cum[:, :, :].rearrange("p i e -> p (i e)"), ps_m[:, 0:NT * N_EXP]))
            for i in range(1, NT):
                link(V.tensor_tensor(cum[:, i, :], cum[:, i, :], cum[:, i - 1, :], ALU.add))
            V.tensor_copy(pfx[:, 0, :], ps_ht[:, 0:N_EXP])
            link(V.tensor_tensor(pfx[:, 1:, :], ps_ht[:, N_EXP:NT * N_EXP].rearrange("p (i e) -> p i e", e=N_EXP),
                                 cum[:, 0:NT - 1, :], ALU.add))
            for b in range(XB):
                dve.wait_ge(xn_out[b], 16 * ((NT + XB - 1 - b) // XB))
            for k in range(2):
                j_k = col[f"jpos{k + 1}"]
                link(V.tensor_tensor(big[:, :, :], msk[:, k], pfx[:, :, :], ALU.mult))
                link(V.reduce_sum(col["pos"][:, :], big[:, :, :], AX.X))
                link(V.tensor_tensor(ge[:, :, :], over_last(col["pos"][:, :], RT - 1),
                                     thr[:, :].unsqueeze(1).to_broadcast([P, NT, RT - 1]), ALU.is_ge))
                link(V.reduce_sum(col["rt"][:, :], ge[:, :, :], AX.X))
                link(V.scalar_tensor_tensor(j_k[:, :], col["rt"][:, :], -float(P), col["pos"][:, :], ALU.mult, ALU.add))
                link(V.tensor_tensor(ohr[:, :, :], over_last(col["rt"][:, :], RT),
                                     iota_r[:, :].unsqueeze(1).to_broadcast([P, NT, RT]), ALU.is_equal))
                link(V.tensor_tensor(msk[:, k], msk[:, k], over_last(code[:, k, :], N_EXP), ALU.mult))
                link(V.tensor_tensor(vk[:, k], ohr[:, :, :].unsqueeze(3).to_broadcast([P, NT, RT, N_EXP]),
                                     msk[:, k].unsqueeze(2).to_broadcast([P, NT, RT, N_EXP]), ALU.mult))
                for i in range(NT):
                    m = k * NT + i
                    if m >= 4:
                        dve.wait_ge(slot_mm, m - 3)
                    V.tensor_scalar(oh_slot[:, m % 4, :], iota_m[:, :], j_k[:, i:i + 1], None,
                                    ALU.is_equal).then_inc(oh_done, 1)
            f3 = act_f[:, :].rearrange("p (r e) -> p r e", e=N_EXP)
            link(V.tensor_tensor(f3, cum[:, NT - 1, :].unsqueeze(1).to_broadcast([P, RT - 1, N_EXP]),
                                 thr[:, :].unsqueeze(2).to_broadcast([P, RT - 1, N_EXP]), ALU.is_gt))
            link(V.tensor_tensor_scan(act_p[:, :], ones_r[:, :], act_f[:, :], 0.0, ALU.mult, ALU.add))
            link(V.scalar_tensor_tensor(act_o[:, :], act_p[:, :], iota_p1[:, :], act_f[:, :],
                                        ALU.is_equal, ALU.mult))
            link(V.tensor_tensor(act_f[:, :], act_o[:, :], iota_c[:, N_EXP:], ALU.mult))
            link(V.reduce_sum(over[:, 0:1], act_f[:, :], AX.X))
            link(V.tensor_tensor(act_o[:, :].rearrange("p (r e) -> p r e", e=N_EXP),
                                 act_o[:, :].rearrange("p (r e) -> p r e", e=N_EXP),
                                 iota_c[:, 0:N_EXP].unsqueeze(1).to_broadcast([P, RT - 1, N_EXP]), ALU.mult))
            V.reduce_sum(over[:, 1:2], act_o[:, :], AX.X).then_inc(over_ready, 1)
            dve.wait_ge(slot_mm, 2 * NT)
            link(V.tensor_scalar(slot_f[:, :], ps_g[:, 0:COLS], 0.0, float(NO_TOKEN), ALU.is_equal, ALU.mult))
            link(V.scalar_tensor_tensor(idx_out[:, :], ps_g[:, 0:COLS], -1.0, slot_f[:, :], ALU.add, ALU.add))
            link(V.tensor_single_scalar(idx_in[:, :], idx_out[:, :], 1, ALU.logical_shift_right))
            dve.wait_ge(over_t, 1)
            link(V.tensor_copy(tile_col[0:1, N_EXP:], ps_ht[0:1, 0:N_EXP]))
            link(V.tensor_copy(tile_exp[0:1, N_EXP:], ps_ht[0:1, P:P + N_EXP]))
            V.tensor_copy(n_more[0:1, :], act_p[0:1, COLS - N_EXP - 1:COLS - N_EXP]).then_inc(list_ready, 1)

            dve.wait_ge(list_ready, 1)
            n_q = dve.value_load(n_more[0:1, 0:1], min_val=0, max_val=N_EXP) + N_EXP

            def split_lo(number, k, slot):
                dve.wait_ge(hi_done, number + 1)
                V.tensor_tensor(lo[:, slot, :], raw[:, k, :], hi[:, slot, :].bitcast(F32),
                                ALU.subtract).then_inc(lo_done, 1)

            def x_lo_part(e):
                dve.wait_ge(xt_hi, e + 1)
                V.tensor_tensor(x_lo[:, :, :].rearrange("p c m -> p (c m)"), ps_xt[:, :],
                                x_hi[:, :, :].bitcast(F32).rearrange("p c m -> p (c m)"),
                                ALU.subtract).then_inc(xt_lo, 1)

            def hidden(e):
                dve.wait_ge(silu_done, e + 1)
                dve.wait_ge(w_used, 6 if isinstance(e, int) and e == 0 else e * 6 + 4)
                V.tensor_tensor(hid[:, :], ps_u[:, :], silu[:, :], ALU.mult).then_inc(hid_done, 1)

            def hidden_lo_part(e):
                dve.wait_ge(ht_hi, e + 1)
                V.tensor_tensor(h_lo[:, :, :].rearrange("p c m -> p (c m)"), ps_ht[:, :],
                                h_hi[:, :, :].bitcast(F32).rearrange("p c m -> p (c m)"),
                                ALU.subtract).then_inc(ht_lo, 1)

            x_lo_part(0)
            dve.wait_ge(lo_done, first_pieces(2) + 1)
            split_lo(first_pieces(3), 3, first_pieces(3) % 3)
            x_lo_part(1)
            hidden(0)
            for k in range(3):
                split_lo(6 + k, k, k)
            hidden_lo_part(0)
            with dve.Fori(1, n_q - 1) as e:
                for k in (3, 4, 5):
                    split_lo(e * 6 + k, k, k % 3)
                x_lo_part(e + 1)
                dve.wait_ge(ht_mm, e)
                hidden(e)
                for k in range(3):
                    split_lo(e * 6 + 6 + k, k, k)
                hidden_lo_part(e)
            for k in (3, 4, 5):
                split_lo(n_q * 6 - 6 + k, k, k % 3)
            dve.wait_ge(ht_mm, n_q - 1)
            hidden(n_q - 1)
            for k in range(2):
                split_lo(n_q * 6 + k, 4 + k, k)
            hidden_lo_part(n_q - 1)
            def final_scale(i):
                if i == 0:
                    dve.wait_ge(gain_in, 32)
                dve.wait_ge(fin_rstd, i + 1)
                V.scalar_tensor_tensor(h[:, i, :], h[:, i, :], rstd[:, i:i + 1], gain, ALU.mult,
                                       ALU.mult).then_inc(fin_done, 1)

            for i in range(NT):
                n = tile_rows(i)
                dve.wait_ge(yc_in[i % NB], 16 * (i // NB + 1))
                for k in range(2):
                    V.scalar_tensor_tensor(h[0:n, i, :], yc[0:n, i % NB, k, :], gates[0:n, k, i:i + 1],
                                           h[0:n, i, :], ALU.mult, ALU.add).then_inc(h_new, 1)
                    dve.wait_ge(h_new, 2 * i + k + 1)
                if last_layer and i >= 2:
                    final_scale(i - 2)
            if last_layer:
                for i in range(NT - 2, NT):
                    final_scale(i)

        @block.tensor
        def _(pe):
            T = nc.tensor
            pe.wait_ge(ident_step, 2)
            pe.wait_ge(rt_in, 32)

            def tile_logits(i):
                n = tile_rows(i)
                pe.wait_ge(xt_cp_r, i + 1)
                if i:
                    pe.wait_ge(lg_done, i)
                for c in range(DC):
                    last = T.matmul(ps_m[0:n, 0:N_GRP + N_EXP], xt_r[:, i % 2, c, 0:n], w_rt[:, c, :],
                                    start=(c == 0), stop=(c == DC - 1))
                last.then_inc(lg_mm, 1)

            for i in range(NT):
                n = tile_rows(i)
                pe.wait_ge(xn_done, i + 1)
                if i >= 2:
                    pe.wait_ge(xt_cp_r, i - 1)
                for c in range(DC):
                    last = T.transpose(ps_r[i % 2][:, c * P:c * P + n],
                                       xn[0:n, i % XB, :].rearrange("p (m c) -> p c m", c=DC)[:, c, :],
                                       ident[0:n, 0:n])
                last.then_inc(xt_mm_r, 1)
                if i >= 1:
                    tile_logits(i - 1)
            tile_logits(NT - 1)
            pe.wait_ge(mask_ready, 1)
            pe.wait_ge(consts_set, 4)
            pe.wait_ge(lg_done, NT)
            m2 = msum[:, :, :].rearrange("p i e -> p (i e)")
            T.matmul(ps_ht[:, 0:NT * N_EXP], tri[:], m2, start=True, stop=True)
            T.matmul(ps_m[:, 0:NT * N_EXP], ones[:], m2, start=True, stop=True).then_inc(pfx_mm, 1)
            for m in range(2 * NT):
                i, k = m % NT, m // NT
                pe.wait_ge(oh_done, m + 1)
                T.matmul(ps_g[:, 0:COLS], oh_slot[:, m % 4, :], vk[:, k, i].rearrange("p r e -> p (r e)"),
                         start=(m == 0), stop=(m == 2 * NT - 1)).then_inc(slot_mm, 1)
            pe.wait_ge(over_ready, 1)
            T.transpose(ps_ht[0:1, 0:P], over[:, 0:1], ident[:])
            T.transpose(ps_ht[0:1, P:2 * P], over[:, 1:2], ident[:]).then_inc(over_t, 1)
            pe.wait_ge(list_ready, 1)
            n_q = pe.value_load(n_more[0:1, 0:1], min_val=0, max_val=N_EXP) + N_EXP

            def transpose_x(e):
                pe.wait_ge(xg_in, e * 16 + 16)
                for c in range(DC):
                    last = T.transpose(ps_xt[:, c * P:(c + 1) * P],
                                       xg[:, :].rearrange("p (m c) -> p c m", c=DC)[:, c, :], ident[:])
                last.then_inc(xt_mm, 1)

            def transpose_hidden(e):
                pe.wait_ge(hid_done, e + 1)
                for c in range(FC):
                    last = T.transpose(ps_ht[:, c * P:(c + 1) * P],
                                       hid[:, :].rearrange("p (m c) -> p c m", c=FC)[:, c, :], ident[:])
                last.then_inc(ht_mm, 1)

            def products(out, x_h, x_l, w_h, w_l, first, final):
                T.matmul(out, x_h, w_h, start=first, stop=False)
                T.matmul(out, x_l, w_h, start=False, stop=False)
                return T.matmul(out, x_h, w_l, start=False, stop=final)

            def gate_up(e, number, slots):
                pe.wait_ge(xt_lo, e + 1)
                for k in range(4):
                    pe.wait_ge(lo_done, number(k) + 1)
                    dst = ps_g if k < 2 else ps_u
                    for c in range(KC):
                        cc = KC * (k % 2) + c
                        last = products(dst[:, :], x_hi[:, cc, :], x_lo[:, cc, :],
                                        hi[:, slots[k], c * F:(c + 1) * F], lo[:, slots[k], c * F:(c + 1) * F],
                                        cc == 0, cc == DC - 1)
                    last.then_inc(w_used, 3 if isinstance(number(k), int) and number(k) == 2 else 1)

            def down(e, number, slots=(1, 2)):
                pe.wait_ge(ht_lo, e + 1)
                for k in range(2):
                    pe.wait_ge(lo_done, number(k) + 1)
                    s = slots[k]
                    for c in range(FW):
                        cc = FW * k + c
                        for half in range(2):
                            w = slice(c * D + 512 * half, c * D + 512 * half + 512)
                            last = products(ps_y[:, 512 * half:512 * half + 512], h_hi[:, cc, :], h_lo[:, cc, :],
                                            hi[:, s, w], lo[:, s, w], cc == 0, cc == FC - 1)
                    last.then_inc(w_used, 1)

            transpose_x(0)
            gate_up(0, lambda k: 2 + k, [(2 + k) % 3 for k in range(4)])
            transpose_x(1)
            transpose_hidden(0)
            with pe.Fori(1, n_q - 1) as e:
                gate_up(e, lambda k: e * 6 + k, [k % 3 for k in range(4)])
                transpose_x(e + 1)
                down(e - 1, lambda k: e * 6 + 4 + k)
                transpose_hidden(e)
            gate_up(n_q - 1, lambda k: n_q * 6 - 6 + k, [k % 3 for k in range(4)])
            down(n_q - 2, lambda k: n_q * 6 - 2 + k)
            transpose_hidden(n_q - 1)
            pe.wait_ge(y_done, n_q - 1)
            down(n_q - 1, lambda k: n_q * 6 + k, slots=(0, 1))


DH = 64
N_KV = 4
N_HEADS = D // DH
KV = N_KV * DH
NEG = -1e30
SC_W = N_META + 2 * P
TOK = XT * P + N_META


def phase_project(nc, t):
    NT = XT + 1
    NP = 2 * KV // P + DC
    K_P, V_P = KV // P, 2 * KV // P
    h, q_t, k_t, v_sb = t["h"], t["q_t"], t["k_t"], t["v_sb"]
    w_kv = t["w_kv"].rearrange("(p c) f -> p c f", c=DC)
    w_q = t["w_q"][0].rearrange("(p c) f -> p c f", c=DC)
    with ExitStack() as ctx:
        def sb(name, shape, dt=F32):
            return ctx.enter_context(nc.sbuf_tensor("prj_" + name, shape, dt))

        sem = semaphore_source(nc, ctx, "prj_")

        ident = sb("ident", [P, P])
        mhalf = sb("mhalf", [P, 1])
        sq = sb("sq", [P, D])
        xn = sb("xn", [P, 2, D])
        ss = sb("ss", [P, NT])
        rstd = sb("rstd", [P, NT])
        x_hi, x_lo = (sb(f"x_{x}", [P, DC, TOK], F32R) for x in ("hi", "lo"))
        g_kv, g_q = (sb(x, [P, DC]) for x in ("g_kv", "g_q"))
        raw = sb("raw", [P, 3, DC, P])
        w_hi, w_lo = (sb(f"w_{x}", [P, 2, DC, P], F32R) for x in ("hi", "lo"))
        bk = sb("bk", [P, K_P])
        bq = sb("bq", [P, DC])
        bv = sb("bv", [P, KV])
        ps_x = ctx.enter_context(nc.psum_tensor("prj_ps_x", [P, 2, D], F32))
        acc = ctx.enter_context(nc.psum_tensor("prj_acc", [P, 4, 512], F32))

        w_in = [sem(f"w_in{b}") for b in range(3)]
        gains_in, bias_in, k_copied = (sem(x) for x in ("gains_in", "bias_in", "k_copied"))
        const_set, ident_step, squares_done, ss_scaled, rstd_done, xn_done, xt_mm, xt_hi, xt_lo = (
            sem(x) for x in ("const_set", "ident_step", "squares_done", "ss_scaled", "rstd_done", "xn_done",
                             "xt_mm", "xt_hi", "xt_lo"))
        gained, w_hi_done, w_lo_done, acc_done, acc_free = (
            sem(x) for x in ("gained", "w_hi_done", "w_lo_done", "acc_done", "acc_free"))

        def jobs(n):
            if n < K_P:
                return [(0, 512), (512, 512), (XT * P, N_META)]
            if n < V_P:
                return [(i * P, tile_rows(i)) for i in range(NT)] if n == V_P - 1 else []
            return [(0, 512), (512, 512)]

        def jobs_before(n):
            return sum(len(jobs(m)) for m in range(n))

        block = ctx.enter_context(nc.Block())

        @block.sync
        def _(sp):
            def load(n):
                src = w_kv[:, :, n * P:(n + 1) * P] if n < V_P else w_q[:, :, (n - V_P) * P:(n - V_P + 1) * P]
                sp.dma_start(raw[:, n % 3], src).then_inc(w_in[n % 3], 16)

            for dst, src in ((g_kv, t["norm_kv"]), (g_q, t["norm_mix"][1])):
                sp.dma_start(dst[:, :], src.rearrange("(p c) -> p c", c=DC)).then_inc(gains_in, 16)
            for n in range(3):
                load(n)
            sp.dma_start(bk[:, :], t["b_kv"][0:KV].rearrange("(c p) -> p c", p=P),
                         allow_slow_non_contiguous=True).then_inc(bias_in, 16)
            sp.dma_start(bq[:, :], t["b_q"][0].rearrange("(c p) -> p c", p=P),
                         allow_slow_non_contiguous=True).then_inc(bias_in, 16)
            sp.dma_start(bv[:, :], t["b_kv"][KV:].partition_broadcast(P)).then_inc(bias_in, 16)
            for n in range(3, NP):
                sp.wait_ge(w_lo_done, n - 2)
                load(n)
                if n == V_P:
                    sp.wait_ge(acc_free, jobs_before(K_P))
                    for kv in range(N_KV):
                        r = kv % 2
                        sp.dma_start(k_t[(1 - r) * DH:(2 - r) * DH, kv, :],
                                     k_t[r * DH:(r + 1) * DH, kv, :]).then_inc(k_copied, 16)
            sp.wait_ge(k_copied, 16 * N_KV)

        @block.gpsimd
        def _(pool):
            nc.gpsimd.memset(mhalf[:], -0.5).then_inc(const_set, 1)
            make_identity(nc, pool, ident, ident_step)
            pool.wait_ge(const_set, 1)
            pool.wait_ge(gains_in, 32)

            def gain(n):
                g = g_kv if n < V_P else g_q
                pool.wait_ge(w_in[n % 3], 16 * (n // 3 + 1))
                nc.gpsimd.tensor_tensor(raw[:, n % 3], raw[:, n % 3],
                                        g[:, :].unsqueeze(2).to_broadcast([P, DC, P]), ALU.mult).then_inc(gained, 1)

            for i in range(NT):
                n = tile_rows(i)
                pool.wait_ge(squares_done, i + 1)
                nc.gpsimd.tensor_scalar(ss[0:n, i:i + 1], ss[0:n, i:i + 1], 1.0 / D, EPS,
                                        ALU.mult, ALU.add).then_inc(ss_scaled, 1)
                pool.wait_ge(ss_scaled, i + 1)
                nc.gpsimd.tensor_tensor(rstd[0:n, i:i + 1], ss[0:n, i:i + 1], mhalf[0:n, :],
                                        ALU.pow).then_inc(rstd_done, 1)
                if i < 3:
                    gain(i)
            for n in range(3, NP):
                gain(n)

        @block.scalar
        def _(act):
            def squares(i):
                n = tile_rows(i)
                if i:
                    act.wait_ge(squares_done, i)
                nc.scalar.activation(sq[0:n], h[0:n, i, :], ACT.Square,
                                     accum_out=ss[0:n, i:i + 1]).then_inc(squares_done, 1)

            def split_w(n):
                act.wait_ge(gained, n + 1)
                if n >= 2:
                    act.wait_ge(acc_done, jobs_before(V_P if K_P <= n - 2 < V_P else n - 1))
                nc.scalar.copy(w_hi[:, n % 2], raw[:, n % 3]).then_inc(w_hi_done, 1)

            squares(0)
            for i in range(NT):
                n = tile_rows(i)
                if i + 1 < NT:
                    squares(i + 1)
                act.wait_ge(xt_mm, i + 1)
                nc.scalar.copy(x_hi[:, :, i * P:i * P + n],
                               ps_x[:, i % 2, :].rearrange("p (c m) -> p c m", c=DC)[:, :, 0:n]).then_inc(xt_hi, 1)
            for n in range(NP):
                split_w(n)

        @block.vector
        def _(dve):
            V = nc.vector

            def split_w(n):
                dve.wait_ge(w_hi_done, n + 1)
                V.tensor_tensor(w_lo[:, n % 2], raw[:, n % 3], w_hi[:, n % 2].bitcast(F32),
                                ALU.subtract).then_inc(w_lo_done, 1)

            def lo_part(i):
                n = tile_rows(i)
                dve.wait_ge(xt_hi, i + 1)
                V.tensor_tensor(x_lo[:, :, i * P:i * P + n],
                                ps_x[:, i % 2, :].rearrange("p (c m) -> p c m", c=DC)[:, :, 0:n],
                                x_hi[:, :, i * P:i * P + n].bitcast(F32), ALU.subtract).then_inc(xt_lo, 1)

            for i in range(NT):
                n = tile_rows(i)
                dve.wait_ge(rstd_done, i + 1)
                if i >= 2:
                    dve.wait_ge(xt_mm, i - 1)
                V.tensor_scalar(xn[0:n, i % 2, :], h[0:n, i, :], rstd[0:n, i:i + 1], None,
                                ALU.mult).then_inc(xn_done, 1)
                if i >= 1:
                    lo_part(i - 1)
            lo_part(NT - 1)
            split_w(0)
            dve.wait_ge(bias_in, 48)
            k = 0
            for n in range(NP):
                ahead = n + 1 < NP and n != V_P - 1
                if ahead:
                    split_w(n + 1)
                for at, m in jobs(n):
                    dve.wait_ge(acc_done, k + 1)
                    a = acc[:, k % 4, :]
                    if n < K_P:
                        for r in range(2):
                            rows = slice(r * DH, (r + 1) * DH)
                            last = V.tensor_scalar(k_t[rows, 2 * n + r, at:at + m], a[rows, 0:m],
                                                   bk[rows, n:n + 1], None, ALU.add)
                    elif n < V_P:
                        last = V.tensor_tensor(v_sb[0:m, at // P, :], a[0:m, 0:KV], bv[0:m, :], ALU.add)
                    else:
                        last = V.tensor_scalar(q_t[:, n - V_P, at:at + m], a[:, 0:m], bq[:, n - V_P:n - V_P + 1],
                                               DH ** -0.5, ALU.add, ALU.mult)
                    last.then_inc(acc_free, 1)
                    k += 1
                if n == V_P - 1:
                    split_w(n + 1)

        @block.tensor
        def _(pe):
            T = nc.tensor
            pe.wait_ge(ident_step, 2)
            for i in range(NT):
                n = tile_rows(i)
                pe.wait_ge(xn_done, i + 1)
                if i >= 2:
                    pe.wait_ge(xt_lo, i - 1)
                for c in range(DC):
                    last = T.transpose(ps_x[:, i % 2, c * P:c * P + n],
                                       xn[0:n, i % 2, :].rearrange("p (m c) -> p c m", c=DC)[:, c, :],
                                       ident[0:n, 0:n])
                last.then_inc(xt_mm, 1)
            pe.wait_ge(xt_lo, NT)
            k = 0
            for n in range(NP):
                pe.wait_ge(w_lo_done, n + 1)
                for at, m in jobs(n):
                    if k >= 4:
                        pe.wait_ge(acc_free, k - 3)
                    for c in range(DC):
                        xh, xl = x_hi[:, c, at:at + m], x_lo[:, c, at:at + m]
                        wh, wl = w_hi[:, n % 2, c, :], w_lo[:, n % 2, c, :]
                        if K_P <= n < V_P:
                            wh, wl = w_hi[:, :, c, :], w_lo[:, :, c, :]
                            out = acc[0:m, k % 4, 0:KV].rearrange("p (b f) -> p b f", b=2)
                            pairs = ((xh, wh), (xl, wh), (xh, wl))
                        else:
                            out, pairs = acc[:, k % 4, 0:m], ((wh, xh), (wh, xl), (wl, xh))
                        for s, (stationary, moving) in enumerate(pairs):
                            last = T.matmul(out, stationary, moving, start=(c == 0 and s == 0),
                                            stop=(c == DC - 1 and s == 2))
                    last.then_inc(acc_done, 1)
                    k += 1


def phase_attend(nc, t):
    H2 = 2
    NS = XT * DC
    h, q_t, k_t, v_sb = t["h"], t["q_t"], t["k_t"], t["v_sb"]
    with ExitStack() as ctx:
        def sb(name, shape, dt=F32):
            return ctx.enter_context(nc.sbuf_tensor("att_" + name, shape, dt))

        def ps(name, shape):
            return ctx.enter_context(nc.psum_tensor("att_" + name, shape, F32))

        sem = semaphore_source(nc, ctx, "att_")

        ident = sb("ident", [P, P])
        mask = sb("mask", [P, SC_W])
        sinks = sb("sinks", [P, N_HEADS])
        b_o = sb("b_o", [P, D])
        raw = sb("raw", [P, 2, D])
        wo_hi, wo_lo = (sb(f"wo_{x}", [P, DC, D], F32R) for x in ("hi", "lo"))
        sm = sb("sm", [P, 2, H2, 1 + SC_W])
        nm = sb("nm", [P, 2, H2])
        pr = sb("pr", [P, 2, H2, 1 + SC_W])
        rs = sb("rs", [P, 2, H2])
        rinv = sb("rinv", [P, 2, H2])
        diag = sb("diag", [P, 2, H2, P])
        pt = sb("pt", [P, 2, H2, 3 * P])
        o_hi, o_lo = (sb(f"o_{x}", [P, 2, DC, P], F32R) for x in ("hi", "lo"))
        ps_s = ps("ps_s", [P, 4, 512])
        ps_t = ps("ps_t", [P, H2, 512])
        ps_o = ps("ps_o", [P, 512])
        ps_y = ps("ps_y", [P, 512])

        w_in = [sem(f"w_in{b}") for b in range(2)]
        small_in, bo_in, ident_step, mask_step, sink_set, bo_added, w_hi_done, w_lo_done = (
            sem(x) for x in ("small_in", "bo_in", "ident_step", "mask_step", "sink_set", "bo_added", "w_hi_done",
                             "w_lo_done"))
        sc_mm, sm_done, nm_done, exp_done, rinv_done, diag_done, pt_mm, pt_done, pv_mm, o_hi_done, o_lo_done, y_mm, h_done = (
            sem(x) for x in ("sc_mm", "sm_done", "nm_done", "exp_done", "rinv_done", "diag_done", "pt_mm",
                             "pt_done", "pv_mm", "o_hi_done", "o_lo_done", "y_mm", "h_done"))

        def width(s):
            return SC_W if s >= DC else N_META + P

        block = ctx.enter_context(nc.Block())

        @block.sync
        def _(sp):
            sp.dma_start(sinks[:, :], t["attn_sinks"][0].partition_broadcast(P)).then_inc(small_in, 16)
            sp.dma_start(b_o[:, :], t["b_o"][0].partition_broadcast(P)).then_inc(bo_in, 16)
            for c in range(DC):
                if c >= 2:
                    sp.wait_ge(w_lo_done, c - 1)
                sp.dma_start(raw[:, c % 2, :], t["w_o"][0][c * P:(c + 1) * P, :]).then_inc(w_in[c % 2], 16)

        @block.gpsimd
        def _(pool):
            make_identity(nc, pool, ident, ident_step)
            G_ = nc.gpsimd
            G_.memset(mask[:], 0.0).then_inc(mask_step, 1)
            pool.wait_ge(mask_step, 1)
            G_.affine_select(out=mask[:, N_META:N_META + P], in_=mask[:, N_META:N_META + P], compare_op=ALU.is_ge,
                             fill=NEG, base=0, pattern=[[-1, P]], channel_multiplier=1).then_inc(mask_step, 1)
            G_.affine_select(out=mask[:, N_META + P:], in_=mask[:, N_META + P:], compare_op=ALU.is_gt,
                             fill=NEG, base=0, pattern=[[1, P]], channel_multiplier=-1).then_inc(mask_step, 1)
            pool.wait_ge(small_in, 16)
            for s in range(NS):
                c, i = s % DC, s // DC
                if s >= 2:
                    pool.wait_ge(exp_done, 2 * (s - 1))
                G_.tensor_copy(sm[:, s % 2, :, 0:1], sinks[:, 2 * c:2 * c + 2].unsqueeze(2)).then_inc(sink_set, 1)
                if c == 1:
                    if i == 0:
                        pool.wait_ge(bo_in, 16)
                    G_.tensor_tensor(h[:, i, :], h[:, i, :], b_o[:, :], ALU.add).then_inc(bo_added, 1)

        @block.scalar
        def _(act):
            A = nc.scalar

            def exps(s):
                act.wait_ge(nm_done, s + 1)
                if s >= 2:
                    act.wait_ge(pt_mm, s - 1)
                for r in range(2):
                    A.activation(pr[:, s % 2, r, 0:1 + width(s)], sm[:, s % 2, r, 0:1 + width(s)], ACT.Exp,
                                 bias=nm[:, s % 2, r:r + 1],
                                 accum_out=rs[:, s % 2, r:r + 1]).then_inc(exp_done, 1)

            def copy_weights(s):
                act.wait_ge(pt_mm, s + 1)
                if s >= 2:
                    act.wait_ge(pv_mm, s - 1)
                w = 2 * P if s >= DC else P
                A.copy(pt[:, s % 2, :, 0:w], ps_t[:, :, 0:w])
                A.copy(pt[0:N_META, s % 2, :, 2 * P:], ps_t[0:N_META, :, 2 * P:3 * P]).then_inc(pt_done, 1)

            def o_hi_part(s):
                c, i = s % DC, s // DC
                act.wait_ge(pv_mm, s + 1)
                if i >= 2 and c == 0:
                    act.wait_ge(y_mm, 2 * (i - 1))
                A.copy(o_hi[:, i % 2, c, :], ps_o[:, 0:P]).then_inc(o_hi_done, 1)

            for s in range(NS):
                if s >= 2:
                    o_hi_part(s - 2)
                exps(s)
                if s >= 1:
                    copy_weights(s - 1)
                if s < DC:
                    act.wait_ge(w_in[s % 2], 16 * (s // 2 + 1))
                    A.copy(wo_hi[:, s, :], raw[:, s % 2, :]).then_inc(w_hi_done, 1)
            o_hi_part(NS - 2)
            copy_weights(NS - 1)
            o_hi_part(NS - 1)

        @block.vector
        def _(dve):
            V = nc.vector

            def scores(s):
                dve.wait_ge(sc_mm, s + 1)
                if s >= 2:
                    dve.wait_ge(exp_done, 2 * (s - 1))
                w = width(s)
                V.tensor_tensor(sm[:, s % 2, :, 1:1 + w], ps_s[:, 2 * (s % 2):2 * (s % 2) + 2, 0:w],
                                mask[:, 0:w].unsqueeze(1).to_broadcast([P, H2, w]), ALU.add).then_inc(sm_done, 1)
                dve.wait_ge(sm_done, s + 1)
                dve.wait_ge(sink_set, s + 1)
                V.reduce_max(nm[:, s % 2, :], sm[:, s % 2, :, 0:1 + w], AX.X, negate=True).then_inc(nm_done, 1)

            def divisors(s):
                dve.wait_ge(exp_done, 2 * (s + 1))
                V.reciprocal(rinv[:, s % 2, :], rs[:, s % 2, :]).then_inc(rinv_done, 1)
                dve.wait_ge(rinv_done, s + 1)
                if s >= 2:
                    dve.wait_ge(pt_mm, s - 1)
                V.tensor_tensor(diag[:, s % 2], ident[:, :].unsqueeze(1).to_broadcast([P, H2, P]),
                                rinv[:, s % 2, :].unsqueeze(2).to_broadcast([P, H2, P]),
                                ALU.mult).then_inc(diag_done, 1)

            def o_lo_part(s):
                c, i = s % DC, s // DC
                dve.wait_ge(o_hi_done, s + 1)
                V.tensor_tensor(o_lo[:, i % 2, c, :], ps_o[:, 0:P], o_hi[:, i % 2, c, :].bitcast(F32),
                                ALU.subtract).then_inc(o_lo_done, 1)

            def add_projection(i, half):
                dve.wait_ge(y_mm, 2 * i + half + 1)
                dve.wait_ge(bo_added, i + 1)
                hs = h[:, i, 512 * half:512 * half + 512]
                V.tensor_tensor(hs, hs, ps_y[:, :], ALU.add).then_inc(h_done, 1)

            dve.wait_ge(ident_step, 2)
            dve.wait_ge(mask_step, 3)
            scores(0)
            for s in range(NS):
                c, i = s % DC, s // DC
                if s >= 2:
                    o_lo_part(s - 2)
                divisors(s)
                if s + 1 < NS:
                    scores(s + 1)
                if s < DC:
                    dve.wait_ge(w_hi_done, s + 1)
                    V.tensor_tensor(wo_lo[:, s, :], raw[:, s % 2, :], wo_hi[:, s, :].bitcast(F32),
                                    ALU.subtract).then_inc(w_lo_done, 1)
                if i >= 1 and c in (4, 7):
                    add_projection(i - 1, 0 if c == 4 else 1)
            o_lo_part(NS - 2)
            o_lo_part(NS - 1)
            for half in range(2):
                add_projection(XT - 1, half)

        @block.tensor
        def _(pe):
            T = nc.tensor

            def scores(s):
                c, i = s % DC, s // DC
                if s >= 2:
                    pe.wait_ge(sm_done, s - 1)
                for r in range(2):
                    rows = slice(r * DH, (r + 1) * DH)
                    out = ps_s[:, 2 * (s % 2) + r, :]
                    q = q_t[rows, c, i * P:(i + 1) * P]
                    k = k_t[rows, c // 2, :]
                    T.matmul(out[:, 0:N_META], q, k[:, XT * P:TOK], start=True, stop=True)
                    last = T.matmul(out[:, N_META:N_META + P], q, k[:, i * P:(i + 1) * P], start=True, stop=True)
                    if i:
                        last = T.matmul(out[:, N_META + P:SC_W], q, k[:, (i - 1) * P:i * P], start=True, stop=True)
                last.then_inc(sc_mm, 1)

            def transpose_weights(s):
                i = s // DC
                pe.wait_ge(diag_done, s + 1)
                if s:
                    pe.wait_ge(pt_done, s)
                for r in range(2):
                    p, d = pr[:, s % 2, r, :], diag[:, s % 2, r, :]
                    T.matmul(ps_t[:, r, 0:P], p[:, 1 + N_META:1 + N_META + P], d, start=True, stop=True)
                    if i:
                        T.matmul(ps_t[:, r, P:2 * P], p[:, 1 + N_META + P:1 + SC_W], d, start=True, stop=True)
                    last = T.matmul(ps_t[0:N_META, r, 2 * P:3 * P], p[:, 1:1 + N_META], d, start=True, stop=True)
                last.then_inc(pt_mm, 1)

            def outputs(s):
                c, i = s % DC, s // DC
                pe.wait_ge(pt_done, s + 1)
                if s:
                    pe.wait_ge(o_lo_done, s)
                vc = slice((c // 2) * DH, (c // 2 + 1) * DH)
                for r in range(2):
                    out, w = ps_o[r * DH:(r + 1) * DH, 0:P], pt[:, s % 2, r, :]
                    T.matmul(out, v_sb[:, i, vc], w[:, 0:P], start=True, stop=False)
                    if i:
                        T.matmul(out, v_sb[:, i - 1, vc], w[:, P:2 * P], start=False, stop=False)
                    last = T.matmul(out, v_sb[0:N_META, XT, vc], w[0:N_META, 2 * P:], start=False, stop=True)
                last.then_inc(pv_mm, 1)

            def project(i, half):
                pe.wait_ge(o_lo_done, DC * (i + 1))
                if i == 0 and half == 0:
                    pe.wait_ge(w_lo_done, DC)
                if 2 * i + half:
                    pe.wait_ge(h_done, 2 * i + half)
                for c in range(DC):
                    oh, ol = o_hi[:, i % 2, c, :], o_lo[:, i % 2, c, :]
                    wh, wl = (w[:, c, 512 * half:512 * half + 512] for w in (wo_hi, wo_lo))
                    T.matmul(ps_y[:, :], oh, wh, start=(c == 0), stop=False)
                    T.matmul(ps_y[:, :], ol, wh, start=False, stop=False)
                    last = T.matmul(ps_y[:, :], oh, wl, start=False, stop=(c == DC - 1))
                last.then_inc(y_mm, 1)

            scores(0)
            for s in range(NS):
                c, i = s % DC, s // DC
                if s + 1 < NS:
                    scores(s + 1)
                if s >= 1:
                    outputs(s - 1)
                transpose_weights(s)
                if i >= 1 and c in (3, 6):
                    project(i - 1, 0 if c == 3 else 1)
            outputs(NS - 1)
            for half in range(2):
                project(XT - 1, half)


def program(nc, arrays):
    t = {name: nc.dram_tensor(name, a.shape, F32, kind="ExternalInput").ap() for name, a in arrays.items()}
    out = nc.dram_tensor("out", (1, SEQ, D), F32, kind="ExternalOutput").ap()
    for name, shape in (("u_dram", [D, L, NCH]), ("h_dram", [C, G, HW]), ("z_dram", [D, L, NCH]),
                        ("xn_dram0", [T_ALL, D]), ("y_dram0", [2 * T_ALL, D]),
                        ("xn_dram1", [SEQ, D]), ("y_dram1", [2 * SEQ, D])):
        t[name] = nc.dram_tensor(name, shape, F32).ap()
    phase_ssm(nc, t)
    with ExitStack() as ctx:
        t["h"] = ctx.enter_context(nc.sbuf_tensor("h", [P, XT + 1, D], F32))
        phase_glu(nc, t)
        phase_moe(nc, t, 0)
        with ExitStack() as att:
            t["q_t"] = att.enter_context(nc.sbuf_tensor("q_t", [P, DC, SEQ], F32))
            t["k_t"] = att.enter_context(nc.sbuf_tensor("k_t", [P, N_KV, TOK], F32))
            t["v_sb"] = att.enter_context(nc.sbuf_tensor("v_sb", [P, XT + 1, KV], F32))
            phase_project(nc, t)
            phase_attend(nc, t)
        phase_moe(nc, t, 1, out)


def kernel(**inputs):
    from concourse import bacc
    from concourse.bass_utils import run_bass_kernel_spmd

    arrays = {name: np.ascontiguousarray(a) for name, a in inputs.items()}
    nc = bacc.Bacc("TRN2", target_bir_lowering=False, num_devices=1)
    program(nc, arrays)
    results = run_bass_kernel_spmd(nc, [arrays], core_ids=[0])
    return results.results[0]["out"]
```
